# Optimizing a Trainium2 kernel written in Bass

```python
import jax, jax.numpy as jnp
from jax import lax
import numpy as np

D_MODEL = 1024
BATCH = 1
SEQ = 512
DEPTH = 2

RET_HEADS = 4
RET_QK_DIM = D_MODEL // RET_HEADS
RET_V_DIM = 2 * RET_QK_DIM
RET_QK_W = RET_HEADS * RET_QK_DIM
RET_V_W = RET_HEADS * RET_V_DIM
RET_CHUNK = 128
ROPE_BASE = 10000.0
SB_HEADS = 16
SB_DIM = 64
SB_W = SB_HEADS * SB_DIM
SB_BLOCK = 128
D_FF = 4 * D_MODEL
N_MOD = 6
EPS = 1e-6
GN_EPS = 1e-5
IN_SPLITS = (RET_QK_W, RET_QK_W, RET_V_W, RET_V_W, SB_W, SB_W, SB_W, D_MODEL, D_MODEL)
IN_W = sum(IN_SPLITS)

kernel_name = "hybrid_retention_stickbreaking_gated_block"

def _rmsnorm(x, g):
    xf = x.astype(jnp.float32)
    y = xf * lax.rsqrt(jnp.mean(xf * xf, axis=-1, keepdims=True) + EPS)
    return (y * g.astype(jnp.float32)).astype(x.dtype)

def _modulate(h, shift, scale):
    return h * (1.0 + scale[:, None, :]) + shift[:, None, :]

def _heads(t, n_heads):
    b, s, w = t.shape
    return t.reshape(b, s, n_heads, w // n_heads).transpose(0, 2, 1, 3)

def _merge_heads(t):
    b, h, s, d = t.shape
    return t.transpose(0, 2, 1, 3).reshape(b, s, h * d)

def _rotary(t):
    s, d = t.shape[2], t.shape[3]
    half = d // 2
    inv_freq = jnp.power(ROPE_BASE, -jnp.arange(half, dtype=jnp.float32) / half)
    ang = jnp.arange(s, dtype=jnp.float32)[:, None] * inv_freq[None, :]
    cos, sin = jnp.cos(ang), jnp.sin(ang)
    t1, t2 = t[..., :half], t[..., half:]
    return jnp.concatenate([t1 * cos - t2 * sin, t1 * sin + t2 * cos], axis=-1)

def _retention(q, k, v):
    out_dtype = v.dtype
    q = q.astype(jnp.float32)
    k = k.astype(jnp.float32) * (q.shape[-1] ** -0.5)
    v = v.astype(jnp.float32)
    b, h, s, dk = q.shape
    dv = v.shape[-1]
    c = RET_CHUNK
    n = s // c
    log_gamma = jnp.log1p(-jnp.power(2.0, -5.0 - jnp.arange(h, dtype=jnp.float32)))
    idx = jnp.arange(c, dtype=jnp.float32)
    rel = idx[:, None] - idx[None, :]
    decay = jnp.where(rel >= 0, jnp.exp(jnp.maximum(rel, 0.0) * log_gamma[:, None, None]), 0.0)
    xi = jnp.exp((idx + 1.0) * log_gamma[:, None])
    zeta = jnp.exp((c - 1.0 - idx) * log_gamma[:, None])
    gamma_c = jnp.exp(c * log_gamma)

    qc = q.reshape(b, h, n, c, dk)
    kc = k.reshape(b, h, n, c, dk)
    vc = v.reshape(b, h, n, c, dv)
    scores = jnp.einsum('bhncd,bhnmd->bhncm', qc, kc) * decay[None, :, None]
    o_inner = jnp.einsum('bhncm,bhnme->bhnce', scores, vc)

    def step(r, qkv):
        qn, kn, vn = qkv
        cross = jnp.einsum('bhcd,bhde->bhce', qn, r) * xi[None, :, :, None]
        r_new = r * gamma_c[None, :, None, None] + jnp.einsum(
            'bhcd,bhce->bhde', kn * zeta[None, :, :, None], vn)
        return r_new, cross

    r0 = jnp.zeros((b, h, dk, dv), jnp.float32)
    xs = (jnp.moveaxis(qc, 2, 0), jnp.moveaxis(kc, 2, 0), jnp.moveaxis(vc, 2, 0))
    _, o_cross = lax.scan(step, r0, xs)
    o = (o_inner + jnp.moveaxis(o_cross, 0, 2)).reshape(b, h, s, dv)
    mu = jnp.mean(o, axis=-1, keepdims=True)
    var = jnp.mean(jnp.square(o - mu), axis=-1, keepdims=True)
    return ((o - mu) * lax.rsqrt(var + GN_EPS)).astype(out_dtype)

def _stick_breaking(q, k, v):
    out_dtype = v.dtype
    b, h, s, d = q.shape
    nb = s // SB_BLOCK
    kf = k.astype(jnp.float32)
    vf = v.astype(jnp.float32)
    qb = jnp.moveaxis(q.astype(jnp.float32).reshape(b, h, nb, SB_BLOCK, d), 2, 0)
    kpos = jnp.arange(s)
    scale = d ** -0.5

    def block(args):
        qi, i = args
        qpos = i * SB_BLOCK + jnp.arange(SB_BLOCK)
        causal = kpos[None, :] < qpos[:, None]
        z = jnp.einsum('bhtd,bhsd->bhts', qi, kf) * scale
        log_1m_beta = jnp.where(causal, -jax.nn.softplus(z), 0.0)
        rev_incl = lax.cumsum(log_1m_beta, axis=3, reverse=True)
        rev_excl = jnp.concatenate([rev_incl[..., 1:], jnp.zeros_like(rev_incl[..., :1])], axis=-1)
        a = jnp.where(causal, jnp.exp(jax.nn.log_sigmoid(z) + rev_excl), 0.0)
        return jnp.einsum('bhts,bhsd->bhtd', a, vf)

    out = lax.map(block, (qb, jnp.arange(nb)))
    return jnp.moveaxis(out, 0, 2).reshape(b, h, s, d).astype(out_dtype)

def _mixer(h, w_in, w_ret_out, w_sb_out, w_mix_out):
    p = h @ w_in
    offsets = [int(o) for o in np.cumsum(IN_SPLITS)[:-1]]
    rq, rk, rv, rg, sq, sk, sv, ga, gb = jnp.split(p, offsets, axis=-1)
    y_ret = _retention(_rotary(_heads(rq, RET_HEADS)), _rotary(_heads(rk, RET_HEADS)), _heads(rv, RET_HEADS))
    y_a = (jax.nn.silu(rg) * _merge_heads(y_ret)) @ w_ret_out
    y_sb = _stick_breaking(_heads(sq, SB_HEADS), _heads(sk, SB_HEADS), _heads(sv, SB_HEADS))
    y_b = _merge_heads(y_sb) @ w_sb_out
    merged = jax.nn.sigmoid(ga) * y_a + jax.nn.sigmoid(gb) * y_b
    return merged @ w_mix_out

def setup_inputs(seed: int = 0) -> dict:
    key = jax.random.key(seed)
    ks = jax.random.split(key, 16)
    f32 = jnp.float32

    def w(k, shape, fan_in):
        return jax.random.normal(k, shape, f32) * (fan_in ** -0.5)

    def gain(k, shape):
        return 1.0 + 0.02 * jax.random.normal(k, shape, f32)

    return {
        "x": jax.random.normal(ks[0], (BATCH, SEQ, D_MODEL), f32),
        "c": jax.random.normal(ks[1], (BATCH, D_MODEL), f32),
        "norm_mix_g": gain(ks[2], (DEPTH, D_MODEL)),
        "w_in": w(ks[3], (DEPTH, D_MODEL, IN_W), D_MODEL),
        "w_ret_out": w(ks[4], (DEPTH, RET_V_W, D_MODEL), RET_V_W),
        "w_sb_out": w(ks[5], (DEPTH, SB_W, D_MODEL), SB_W),
        "w_mix_out": w(ks[6], (DEPTH, D_MODEL, D_MODEL), D_MODEL),
        "norm_mlp_g": gain(ks[7], (DEPTH, D_MODEL)),
        "w_up": w(ks[8], (DEPTH, D_MODEL, D_FF), D_MODEL),
        "w_down": w(ks[9], (DEPTH, D_FF, D_MODEL), D_FF),
        "w_ada": w(ks[10], (DEPTH, D_MODEL, N_MOD * D_MODEL), D_MODEL),
        "b_ada": 0.02 * jax.random.normal(ks[11], (DEPTH, N_MOD * D_MODEL), f32),
        "final_g": gain(ks[12], (D_MODEL,)),
    }

def reference(x, c, norm_mix_g, w_in, w_ret_out, w_sb_out, w_mix_out, norm_mlp_g,
              w_up, w_down, w_ada, b_ada, final_g):
    c_act = jax.nn.silu(c)
    for l in range(DEPTH):
        mod = c_act @ w_ada[l] + b_ada[l]
        shift1, scale1, gate1, shift2, scale2, gate2 = jnp.split(mod, N_MOD, axis=-1)
        h = _modulate(_rmsnorm(x, norm_mix_g[l]), shift1, scale1)
        x = x + gate1[:, None, :] * _mixer(h, w_in[l], w_ret_out[l], w_sb_out[l], w_mix_out[l])
        h2 = _modulate(_rmsnorm(x, norm_mlp_g[l]), shift2, scale2)
        u = jnp.square(jax.nn.relu(h2 @ w_up[l]))
        x = x + gate2[:, None, :] * (u @ w_down[l])
    return _rmsnorm(x, final_g)


_drawn_inputs = setup_inputs


def setup_inputs(seed=0):
    import zlib

    import numpy as np

    out = dict(_drawn_inputs(seed))
    spreads = {}
    factors = {'norm_mix_g': 3.283, 'norm_mlp_g': 2.876, 'final_g': 2.878}
    for name, (base, spread) in spreads.items():
        noise = np.random.default_rng([zlib.crc32(name.encode()), seed]).standard_normal(out[name].shape)
        drawn = base * np.exp(spread * noise) if base else spread * noise
        out[name] = __import__('jax').numpy.asarray(drawn.astype(out[name].dtype))
    for name, factor in factors.items():
        out[name] = (out[name] * factor).astype(out[name].dtype)
    return out
```

```python
import math
from contextlib import ExitStack, contextmanager

import numpy as np

import concourse.bass as bass
from concourse import mybir

P = 128
D = 1024
SEQ = 512
DEPTH = 2
KT = D // P
TB = SEQ // P
UNIT = 256
IN_W = 11264
RET_HEADS, RET_QK, RET_V = 4, 256, 512
SB_HEADS, SB_DIM = 16, 64
SB_GROUPS = SB_HEADS * SB_DIM // UNIT
D_FF = 4096
QUARTERS = D_FF // D
MODS = 6
SHIFT1, SCALE1, GATE1, SHIFT2, SCALE2, GATE2 = range(MODS)
EPS, GN_EPS = 1e-6, 1e-5
RQ, RK, RV, RG = 0, 1024, 2048, 4096
SQ, SK, SV, GA, GB = 6144, 7168, 8192, 9216, 10240

RET_LOOPS = RET_HEADS // 2
RET_PAIRS = 8
SB_FIRST = RET_LOOPS * RET_PAIRS * 2
SB_LOOP = SB_FIRST + 3
SB_LAST = SB_LOOP + 4 * (SB_GROUPS - 1)
GB_LAST = SB_LAST + 4
SB_OUT = GB_LAST + 1
MIX = SB_OUT + 4
MLP = MIX + 4
LAYER_UNITS = MLP + 8 * QUARTERS
LAYER_PAIRS = LAYER_UNITS // 2
UNITS = DEPTH * LAYER_UNITS
LO_CREDIT = 4

OFF = [0, 512, 1024, 896]
WID = [SEQ - P * j for j in range(TB)]
CAUSAL = sum(WID)
BIG = 3.0e38


class Chain:

    def __init__(self, eng, sem):
        self.eng, self.sem, self.base, self.count = eng, sem, 0, 0

    def mark(self, ins):
        ins.then_inc(self.sem, 1)
        self.count += 1

    def settle(self):
        self.eng.wait_ge(self.sem, self.base + self.count)

    def link(self, ins):
        self.mark(ins)
        self.settle()

    @contextmanager
    def loop(self, times, per):
        base, before = self.base, self.count
        with self.eng.Fori(0, times) as i:
            self.base, self.count = base + before + per * i, 0
            yield i
            assert self.count == per, f"the loop marks {self.count} times, not {per}"
        self.base, self.count = base, before + per * times


def hybrid_trunk(nc, x, c, norm_mix_g, w_in, w_ret_out, w_sb_out, w_mix_out, norm_mlp_g,
                 w_up, w_down, w_ada, b_ada, final_g, rope, decay, out):
    f32, f32r = mybir.dt.float32, mybir.dt.float32r
    ALU, ACT = mybir.AluOpType, mybir.ActivationFunctionType
    ds = bass.ds
    EXP_LN = "natural_log_exp_and_others"

    ctx = ExitStack()
    with ctx:
        def sb(name, shape, dt=f32):
            return ctx.enter_context(nc.sbuf_tensor(name, shape, dt))

        def sem(name):
            return ctx.enter_context(nc.semaphore(name))

        x_T = sb("x_T", [P, KT, SEQ])
        h_hi = sb("h_hi", [P, KT, SEQ], f32r)
        h_lo = sb("h_lo", [P, KT, SEQ], f32r)
        y_hi = sb("y_hi", [P, KT, SEQ], f32r)
        y_lo = sb("y_lo", [P, KT, SEQ], f32r)
        ya = sb("ya", [P, KT, SEQ])
        w_raw = sb("w_raw", [P, 2, KT, UNIT])
        w_hi = sb("w_hi", [P, 4, KT, P], f32r)
        w_lo = sb("w_lo", [P, 4, KT, P], f32r)
        sp_hi = sb("sp_hi", [P, 2, CAUSAL], f32r)
        sp_lo = sb("sp_lo", [P, 2, CAUSAL], f32r)
        ident = sb("ident", [P, P])
        ones = sb("ones", [P, P])
        upto = sb("upto", [P, P])
        neg_f = sb("neg_f", [P, P])
        neg_tri = sb("neg_tri", [P, P], f32r)
        neg_ones = sb("neg_ones", [P, P], f32r)
        rows = sb("rows", [P, P])
        mod = sb("mod", [P, DEPTH * MODS * KT])
        vecs = sb("vecs", [P, 6, KT])
        c_act = sb("c_act", [P, KT])
        n_scale = sb("n_scale", [P, 2 * DEPTH * KT])
        n_shift = sb("n_shift", [P, 2 * DEPTH * KT])
        eps_c = sb("eps_c", [P, 1])
        gn_eps_c = sb("gn_eps_c", [P, 1])
        WORK = 9216
        work = sb("work", [P, WORK])

        def part(at, *shape):
            n = math.prod(shape)
            assert at + n <= WORK
            v = work[:, at:at + n]
            if len(shape) == 2:
                v = v.rearrange("p (a b) -> p a b", a=shape[0])
            if len(shape) == 3:
                v = v.rearrange("p (a b c) -> p a b c", a=shape[0], b=shape[1])
            return v

        ada_raw = part(0, 2, KT, UNIT)
        x_tok = ya[:, :, :].rearrange("p a b -> p (a b)").rearrange("p (t d) -> p t d", t=TB)
        sq = part(0, 2, SEQ)
        sq_sum = part(1024, SEQ)
        rstd = part(1536, SEQ)
        normed = part(2048, 2, SEQ)
        qk = part(0, 4, SEQ)
        v_ret = part(2048, TB, RET_V)
        g_ret = part(4096, TB, SEQ)
        p_ret = part(6144, CAUSAL)
        rope_t = part(7424, 2, SEQ)
        rot = part(8448, SEQ)
        gated_t = rot
        stats = sb("stats", [P, TB, 6])
        moments = sb("moments", [P, TB, 2])
        mean_diff = sb("mean_diff", [P, TB])
        ret_rstd = sb("ret_rstd", [P, TB])
        decay_t = sb("decay_t", [P, SEQ])
        sb_next = part(0, 3, 1024)
        sb_now = part(3072, 3, 1024)
        terms = part(6144, 2, CAUSAL)
        gate_t = part(8704, SEQ)
        sg = part(0, KT, SEQ)
        merged_t = part(4096, 2, SEQ)
        relu_t = part(0, 2, SEQ)
        u_t = part(1024, 2, SEQ)
        y_T = part(3072, KT, SEQ)

        now_k, now_v, now_q = 0, 1, 2

        def tile2(buf, i):
            return buf[:, i, :].rearrange("p (a t) -> p a t", a=2)

        def blocks(buf, i):
            return buf[:, i, :].rearrange("p (s d) -> p s d", s=TB)

        proj = ctx.enter_context(nc.psum_tensor("proj", [P, 2, SEQ], f32))
        att = ctx.enter_context(nc.psum_tensor("att", [P, 6, SEQ], f32))
        att_flat = att[:, :, :].rearrange("p b n -> p (b n)")

        RET_BANKS = [3, 4, 5, 2]
        SB_OUT_BANK = 5

        def scores_of(a):
            return att_flat[:, 3 * a * SEQ:3 * a * SEQ + CAUSAL]

        rows_in, consts_in = sem("rows_in"), sem("consts_in")
        x_in, out_stored = sem("x_in"), sem("out_stored")
        ada_in = [sem("ada_in0"), sem("ada_in1")]
        decay_in, rope_in = sem("decay_in"), sem("rope_in")
        raw_in = [sem("raw_in0"), sem("raw_in1")]
        consts_made, vecs_turned, vecs_ready = sem("consts_made"), sem("vecs_turned"), sem("vecs_ready")
        x_turned, x_ready, x_ready_dve = sem("x_turned"), sem("x_ready"), sem("x_ready_dve")
        c_sig, c_ready, ada_done, mods_ready = sem("c_sig"), sem("c_ready"), sem("ada_done"), sem("mods_ready")
        hi_ready, lo_ready = sem("hi_ready"), sem("lo_ready")
        proj_done = sem("proj_done")
        bank_free = [sem("bank_free0"), sem("bank_free1")]
        squared, sq_used, sq_summed, ms_done, rstd_ready = (
            sem("squared"), sem("sq_used"), sem("sq_summed"), sem("ms_done"), sem("rstd_ready"))
        x_normed, h_half, h_ready = sem("x_normed"), sem("h_half"), sem("h_ready")
        qk_rotated = sem("qk_rotated")
        scores_done, probs_ready, ret_done = sem("scores_done"), sem("probs_ready"), sem("ret_done")
        moments_ready, ret_rstd_ready, ret_normed = (
            sem("moments_ready"), sem("ret_rstd_ready"), sem("ret_normed"))
        ret_turned, ret_gated, sig_ready = sem("ret_turned"), sem("ret_gated"), sem("sig_ready")
        z_done, log_ready, sp_ready = sem("z_done"), sem("log_ready"), sem("sp_ready")
        broken, weights_exp, weights_ready = sem("broken"), sem("weights_exp"), sem("weights_ready")
        sb_done, sb_half, sb_ready = sem("sb_done"), sem("sb_half"), sem("sb_ready")
        next_stored, qk_now, v_now = sem("next_stored"), sem("qk_now"), sem("v_now")
        gate_ready, gate_used, merged_sum, merged_half, merged_ready = (
            sem("gate_ready"), sem("gate_used"), sem("merged_sum"), sem("merged_half"), sem("merged_ready"))
        relu_ready, u_ready, u_half, u_split = sem("relu_ready"), sem("u_ready"), sem("u_half"), sem("u_split")
        y_normed, y_turned, y_stored, y_stored_dve = (
            sem("y_normed"), sem("y_turned"), sem("y_stored"), sem("y_stored_dve"))
        dve_own, act_own = sem("dve_own"), sem("act_own")

        def tiles(w):
            return w.rearrange("l (k p) n -> p l k n", p=P)

        win_v, wret_v, wsb_v, wmix_v, wup_v, wdown_v, wada_v = map(
            tiles, (w_in, w_ret_out, w_sb_out, w_mix_out, w_up, w_down, w_ada))

        block = ctx.enter_context(nc.Block())

        @block.sync
        def _(sp):
            bias_rows = b_ada.rearrange("l (n p) -> (l n) p", p=P)
            sp.dma_start(rows[0:bias_rows.shape[0], :], bias_rows).then_inc(rows_in, 16)
            sp.dma_start(x_tok, x.rearrange("b (t p) d -> p (b t) d", p=P)).then_inc(x_in, 16)
            with sp.Fori(0, DEPTH) as layer:
                with sp.Fori(0, MODS * D // UNIT // 2) as i:
                    for s in range(2):
                        sp.wait_ge(ada_done, layer * 24 + 2 * i + s + 1)
                        sp.dma_start(ada_raw[:, s:s + 1, :, :],
                                     wada_v[:, ds(layer, 1), :, ds(i * 2 * UNIT + s * UNIT, UNIT)]
                                     ).then_inc(ada_in[s], 16)

            def load(pair, unit, src):
                s = unit % 2
                sp.wait_ge(lo_ready, 4 * pair + 2 * unit - 2 + LO_CREDIT)
                sp.dma_start(w_raw[:, s:s + 1, :, :], src).then_inc(raw_in[s], 16)

            with sp.Fori(0, DEPTH) as layer:
                l1 = ds(layer, 1)
                first = layer * LAYER_PAIRS

                def w_in_cols(col):
                    return win_v[:, l1, :, ds(col, UNIT)]

                with sp.Fori(0, RET_LOOPS) as i:
                    pair = first + RET_PAIRS * i
                    for j in range(2):
                        head_qk, head_v = (2 * i + j) * RET_QK, (2 * i + j) * RET_V
                        cols = [RQ + head_qk, RK + head_qk, RV + head_v, RV + UNIT + head_v,
                                RG + head_v, RG + UNIT + head_v]
                        for n, col in enumerate(cols):
                            load(pair, 6 * j + n, w_in_cols(col))
                    for m in range(4):
                        load(pair, 12 + m, wret_v[:, l1, ds(KT * i, KT), m * UNIT:(m + 1) * UNIT])
                for n, col in enumerate([SK, SV, SQ]):
                    load(first, SB_FIRST + n, win_v[:, l1, :, col:col + UNIT])
                with sp.Fori(0, SB_GROUPS - 1) as g:
                    pair = first + 2 * g
                    for n, col in enumerate([GA - UNIT, SK, SV, SQ]):
                        load(pair, SB_LOOP + n, w_in_cols(g * UNIT + (col + UNIT)))
                for n, col in enumerate([GA + 3 * UNIT] + [GB + m * UNIT for m in range(4)]):
                    load(first, SB_LAST + n, win_v[:, l1, :, col:col + UNIT])
                for m in range(4):
                    load(first, SB_OUT + m, wsb_v[:, l1, :, m * UNIT:(m + 1) * UNIT])
                for m in range(4):
                    load(first, MIX + m, wmix_v[:, l1, :, m * UNIT:(m + 1) * UNIT])
                with sp.Fori(0, QUARTERS) as f:
                    pair = first + 4 * f
                    for m in range(4):
                        load(pair, MLP + m, wup_v[:, l1, :, ds(f * D + m * UNIT, UNIT)])
                    for m in range(4):
                        load(pair, MLP + 4 + m, wdown_v[:, l1, ds(KT * f, KT), m * UNIT:(m + 1) * UNIT])

            for t in range(TB):
                sp.wait_ge(y_stored, t + 1)
                sp.wait_ge(y_stored_dve, t + 1)
                sp.dma_start(out[0, t * P:(t + 1) * P, :], x_tok[:, t, :]).then_inc(out_stored, 16)
            sp.wait_ge(out_stored, 16 * TB)

        @block.gpsimd
        def _(pool):
            pool.memset(ident[:, :], 0.0).then_inc(consts_made, 1)
            pool.memset(ones[:, :], 1.0 / D).then_inc(consts_made, 1)
            pool.memset(upto[:, :], BIG).then_inc(consts_made, 1)
            pool.memset(neg_f[:, :], -1.0).then_inc(consts_made, 1)
            pool.wait_ge(consts_made, 4)
            pool.affine_select(out=ident[:, :], in_=ident[:, :], compare_op=ALU.not_equal, fill=1.0,
                               base=0, pattern=[[-1, P]], channel_multiplier=1).then_inc(consts_made, 1)
            pool.affine_select(out=upto[:, :], in_=upto[:, :], compare_op=ALU.is_gt, fill=0.0,
                               base=0, pattern=[[1, P]], channel_multiplier=-1).then_inc(consts_made, 1)
            pool.tensor_copy(neg_ones[:, :], neg_f[:, :]).then_inc(consts_made, 1)
            pool.wait_ge(consts_made, 7)
            pool.affine_select(out=neg_f[:, :], in_=neg_f[:, :], compare_op=ALU.is_ge, fill=0.0,
                               base=0, pattern=[[-1, P]], channel_multiplier=1).then_inc(consts_made, 1)
            pool.wait_ge(consts_made, 8)
            pool.tensor_copy(neg_tri[:, :], neg_f[:, :]).then_inc(consts_made, 1)
            pool.sem_inc(lo_ready, LO_CREDIT)
            with pool.Fori(0, UNITS // 2) as v:
                for s in range(4):
                    pool.wait_ge(hi_ready, 4 * v + s + 1)
                    pool.tensor_tensor(w_lo[:, s, :, :], w_raw[:, s // 2, :, P * (s % 2):P * (s % 2 + 1)],
                                       w_hi[:, s, :, :], ALU.subtract).then_inc(lo_ready, 1)

        @block.scalar
        def _(act):
            own = Chain(act, act_own)
            act.dma_start(decay_t[0:8, 0:P], c.rearrange("b (n p) -> (b n) p", p=P)).then_inc(consts_in, 16)
            act.dma_start(decay_t[8:24, 0:P], norm_mix_g.rearrange("l (n p) -> (l n) p", p=P)).then_inc(consts_in, 16)
            act.dma_start(decay_t[24:40, 0:P], norm_mlp_g.rearrange("l (n p) -> (l n) p", p=P)).then_inc(consts_in, 16)
            act.dma_start(decay_t[40:48, 0:P], final_g.rearrange("(n p) -> n p", p=P)).then_inc(consts_in, 16)
            act.wait_ge(vecs_ready, 1)
            act.activation(c_act[:, :], vecs[:, 0, :], ACT.Sigmoid).then_inc(c_sig, 1)
            act.preload_act_table_set(EXP_LN)
            for k in range(1, KT, 2):
                act.wait_ge(x_turned, k + 1)
                act.activation(x_T[:, k, :], att[:, k % 6, :], ACT.Copy).then_inc(x_ready, 1)

            def split_weights(pair, unit, j):
                s = unit % 2
                act.wait_ge(raw_in[s], 16 * (pair + unit // 2 + 1))
                act.activation(w_hi[:, 2 * s + j, :, :], w_raw[:, s, :, P * j:P * (j + 1)],
                               ACT.Copy).then_inc(hi_ready, 1)

            def products(pair, unit, j):
                act.wait_ge(proj_done, 4 * pair + 2 * unit + j + 1)

            def norm(n, unit):
                act.wait_ge(bank_free[1], unit + 1)
                for k in range(KT):
                    if k >= 2:
                        act.wait_ge(sq_used, 7 * n + max(2, k - 1))
                    act.activation(sq[:, k % 2, :], x_T[:, k, :], ACT.Square).then_inc(squared, 1)
                act.wait_ge(ms_done, n + 1)
                own.link(act.activation(rstd, att[:, 0, :], ACT.Ln, bias=eps_c[:, :]))
                act.activation(rstd, rstd, ACT.Exp, scale=-0.5).then_inc(rstd_ready, 1)

            def norm_affine(n, unit):
                norm(n, unit)
                for k in range(KT):
                    act.wait_ge(x_normed, KT * n + k + 1)
                    own.link(act.activation(normed[:, k % 2, :], normed[:, k % 2, :], ACT.Identity,
                                            bias=n_shift[:, ds(KT * n + k, 1)], scale=n_scale[:, ds(KT * n + k, 1)]))
                    act.activation(h_hi[:, k, :], normed[:, k % 2, :], ACT.Copy).then_inc(h_half, 1)

            def sigmoid(dst, src):
                ins = act.activation(dst, src, ACT.Sigmoid)
                act.preload_act_table_set(EXP_LN)
                return ins

            act.wait_ge(mods_ready, 1)
            act.wait_ge(x_ready, 4)
            act.wait_ge(x_ready_dve, 4)
            with own.loop(DEPTH, 54) as layer:
                first = layer * LAYER_PAIRS
                for unit in range(2):
                    for j in range(2):
                        split_weights(first, unit, j)
                act.dma_start(rope_t, rope).then_inc(rope_in, 16)
                norm_affine(2 * layer, LAYER_UNITS * layer)

                with own.loop(RET_LOOPS, 2) as i:
                    pair = first + RET_PAIRS * i
                    for j in range(2):
                        head = 4 * layer + 2 * i + j
                        u = 6 * j
                        for unit in (u, u + 1):
                            for half in range(2):
                                products(pair, unit, half)
                                if unit == u and half == 0:
                                    act.dma_start(decay_t[:, :], decay[:, ds(2 * i + j, 1), :].rearrange("p a n -> p (a n)")
                                                  ).then_inc(decay_in, 16)
                                split_weights(pair, unit + 2, half)
                        for unit in (u + 2, u + 3):
                            for half in range(2):
                                products(pair, unit, 1)
                                col = UNIT * (unit - u - 2)
                                act.activation(v_ret[:, 2 * half:2 * half + 2, col:col + UNIT],
                                               proj[:, half, :].rearrange("p (a n) -> p a n", a=2),
                                               ACT.Copy).then_inc(bank_free[half], 1)
                                split_weights(pair, unit + 2, half)
                        for n in range(4):
                            if n == 3:
                                act.preload_act_table_set(EXP_LN)
                                act.wait_ge(moments_ready, head + 1)
                                own.link(act.activation(ret_rstd[:, :], moments[:, :, 1], ACT.Ln, bias=gn_eps_c[:, :],
                                                        scale=1.0 / RET_V))
                                act.activation(ret_rstd[:, :], ret_rstd[:, :], ACT.Exp,
                                               scale=-0.5).then_inc(ret_rstd_ready, 1)
                            unit, half = u + 4 + n // 2, n % 2
                            products(pair, unit, half)
                            act.activation(g_ret[:, n, :], proj[:, half, :], ACT.Sigmoid).then_inc(sig_ready, 1)
                            split_weights(pair, unit + 2, half)
                        act.preload_act_table_set(EXP_LN)
                    for unit in range(12, 16):
                        for half in range(2):
                            products(pair, unit, half)
                            split_weights(pair, unit + 2, half)

                def store_feature(pair, unit, half, dst, scale=1.0):
                    products(pair, unit, half)
                    act.activation(dst, proj[:, half, :], ACT.Copy, scale=scale).then_inc(bank_free[half], 1)
                    split_weights(pair, unit + 2, half)

                def store_k(pair, unit, half):
                    store_feature(pair, unit, half, tile2(sb_next, now_k)[:, half, :])

                def store_q(pair, unit, half):
                    store_feature(pair, unit, half, tile2(sb_next, now_q)[:, half, :], SB_DIM ** -0.5)

                def store_v(pair, unit):
                    for half in range(2):
                        products(pair, unit, 1)
                        act.activation(blocks(sb_next, now_v)[:, 2 * half:2 * half + 2, :],
                                       proj[:, half, :].rearrange("p (a n) -> p a n", a=2),
                                       ACT.Copy).then_inc(bank_free[half], 1)
                        split_weights(pair, unit + 2, half)

                def gate(pair, unit, half, dst, done):
                    products(pair, unit, half)
                    sigmoid(dst, proj[:, half, :]).then_inc(done, 1)
                    split_weights(pair, unit + 2, half)

                def logs(n):
                    for a in range(2):
                        act.wait_ge(z_done, 2 * n + a + 1)
                        own.link(act.activation(terms[:, a, :], scores_of(a), ACT.Abs))
                        own.link(act.activation(terms[:, a, :], terms[:, a, :], ACT.Exp, scale=-1.0))
                        act.activation(terms[:, a, :], terms[:, a, :], ACT.Ln, bias=1.0).then_inc(log_ready, 1)

                def weights(n):
                    for a in range(2):
                        act.wait_ge(broken, 2 * n + a + 1)
                        act.wait_ge(sp_ready, 2 * n + a + 1)
                        act.activation(terms[:, a, :], scores_of(a), ACT.Exp).then_inc(weights_exp, 1)

                def head_pair_out(n, tile):
                    act.wait_ge(sb_done, n + 1)
                    act.activation(y_hi[:, tile, :], att[:, SB_OUT_BANK:SB_OUT_BANK + 1, :], ACT.Copy).then_inc(sb_half, 1)

                for half in range(2):
                    store_k(first, SB_FIRST, half)
                store_v(first, SB_FIRST + 1)
                for half in range(2):
                    store_q(first, SB_FIRST + 2, half)

                def group(pair, g, at, last):
                    n = 8 * layer + 2 * g
                    logs(n)
                    for half in range(2):
                        act.wait_ge(gate_used, 8 * layer + 2 * g + half + 1)
                        products(pair, at, half)
                        sigmoid(gate_t, proj[:, half, :]).then_inc(bank_free[half], 1)
                        split_weights(pair, at + 2, half)
                    if last:
                        gate(pair, at + 1, 0, sg[:, 0, :], bank_free[0])
                    else:
                        store_k(pair, at + 1, 0)
                    weights(n)
                    if last:
                        gate(pair, at + 1, 1, sg[:, 1, :], bank_free[1])
                    else:
                        store_k(pair, at + 1, 1)
                    head_pair_out(n, ds(2 * g, 1))
                    logs(n + 1)
                    if last:
                        gate(pair, at + 2, 0, sg[:, 2, :], bank_free[0])
                        gate(pair, at + 2, 1, sg[:, 3, :], bank_free[1])
                        gate(pair, at + 3, 0, sg[:, 4, :], bank_free[0])
                    else:
                        store_v(pair, at + 2)
                        store_q(pair, at + 3, 0)
                    weights(n + 1)
                    if last:
                        gate(pair, at + 3, 1, sg[:, 5, :], bank_free[1])
                    else:
                        store_q(pair, at + 3, 1)
                    head_pair_out(n + 1, ds(2 * g + 1, 1))

                with own.loop(SB_GROUPS - 1, 8) as g:
                    group(first + 2 * g, g, SB_LOOP, False)
                group(first, SB_GROUPS - 1, SB_LAST, True)

                for half in range(2):
                    gate(first, GB_LAST, half, sg[:, 6 + half, :], bank_free[half])
                for m in range(4):
                    for half in range(2):
                        act.wait_ge(merged_sum, KT * layer + 2 * m + half + 1)
                        act.activation(h_hi[:, 2 * m + half, :], merged_t[:, half, :], ACT.Copy).then_inc(merged_half, 1)
                        split_weights(first, SB_OUT + m + 2, half)
                for m in range(4):
                    for half in range(2):
                        products(first, MIX + m, half)
                        split_weights(first, MIX + m + 2, half)
                norm_affine(2 * layer + 1, LAYER_UNITS * layer + MLP)

                def up(pair, f):
                    for m in range(4):
                        for half in range(2):
                            k = 2 * m + half
                            products(pair, MLP + m, half)
                            act.activation(relu_t[:, half, :], proj[:, half, :], ACT.Relu).then_inc(bank_free[half], 1)
                            act.wait_ge(u_ready, KT * (4 * layer + f) + k + 1)
                            act.activation(y_hi[:, k, :], u_t[:, half, :], ACT.Copy).then_inc(u_half, 1)
                            split_weights(pair, MLP + m + 2, half)

                def down(pair, ahead):
                    for m in range(4):
                        for half in range(2):
                            products(pair, MLP + 4 + m, half)
                            if m < ahead:
                                split_weights(pair, MLP + 4 + m + 2, half)

                with own.loop(QUARTERS - 1, 0) as f:
                    up(first + 4 * f, f)
                    down(first + 4 * f, 4)
                last = first + 4 * (QUARTERS - 1)
                up(last, QUARTERS - 1)
                down(last, 2)

            norm(2 * DEPTH, UNITS)
            for k in range(KT):
                act.wait_ge(x_normed, KT * 2 * DEPTH + k + 1)
                act.activation(y_T[:, k, :], y_T[:, k, :], ACT.Copy,
                               scale=vecs[:, 5, k:k + 1]).then_inc(y_normed, 1)
            for t in range(TB):
                act.wait_ge(y_turned, 2 * t + 2)
                act.activation(x_tok[:, t, SEQ:2 * SEQ], att[:, 2 * (t % 3) + 1, :], ACT.Copy).then_inc(y_stored, 1)

        @block.tensor
        def _(pe):
            n_rows = DEPTH * MODS * KT
            pe.wait_ge(consts_made, 9)
            pe.wait_ge(rows_in, 16)
            pe.wait_ge(consts_in, 64)
            pe.transpose(att[:, 0, 0:n_rows], rows[0:n_rows, :], ident[0:n_rows, 0:n_rows])
            pe.transpose(att[:, 0, n_rows:n_rows + 6 * KT], decay_t[0:6 * KT, 0:P],
                         ident[0:6 * KT, 0:6 * KT]).then_inc(vecs_turned, 1)
            pe.wait_ge(x_in, 16)
            for k in range(KT):
                if k == 0:
                    pe.wait_ge(vecs_ready, 1)
                if k >= 6:
                    pe.wait_ge(x_ready_dve if k % 2 == 0 else x_ready, 1)
                for t in range(TB):
                    last = pe.transpose(att[:, k % 6, t * P:(t + 1) * P], x_tok[:, t, k * P:(k + 1) * P], ident[:, :])
                last.then_inc(x_turned, 1)
            pe.wait_ge(c_ready, 1)
            pe.sem_inc(ada_done, 2)
            ada = proj[:, 0, 0:n_rows]
            units = MODS * D // UNIT
            with pe.Fori(0, DEPTH) as layer:
                with pe.Fori(0, units // 2) as i:
                    for s in range(2):
                        pe.wait_ge(ada_in[s], 16 * (layer * (units // 2) + i + 1))
                        for j in range(2):
                            for k in range(KT):
                                last = pe.matmul(ada[:, ds(layer * 2 * units + i * 4 + 2 * s + j, 1)],
                                                 ada_raw[:, s, k, j * P:(j + 1) * P], c_act[:, k:k + 1],
                                                 start=k == 0, stop=k == KT - 1)
                        last.then_inc(ada_done, 1)
            pe.wait_ge(mods_ready, 1)

            def half_unit(pair, unit, j, hi, lo, tile_ready=None):
                slot = 2 * (unit % 2) + j
                pe.wait_ge(lo_ready, 4 * pair + 2 * unit + j + 1 + LO_CREDIT)
                pe.wait_ge(bank_free[j], 2 * pair + unit + 1)
                for k in range(KT):
                    if tile_ready:
                        tile_ready(k)
                    for n, (w, a) in enumerate(((w_hi, hi), (w_hi, lo), (w_lo, hi))):
                        last = pe.matmul(proj[:, j, :], w[:, slot, k, :], a[:, k, :],
                                         start=k == 0 and n == 0, stop=k == KT - 1 and n == 2)
                last.then_inc(proj_done, 1)

            def whole_unit(pair, unit, hi, lo, tile_ready=None):
                for j in range(2):
                    half_unit(pair, unit, j, hi, lo, tile_ready if j == 0 else None)

            def token_unit(pair, unit):
                slot = 2 * (unit % 2)
                pe.wait_ge(lo_ready, 4 * pair + 2 * unit + 2 + LO_CREDIT)
                for t in range(TB):
                    if t % 2 == 0:
                        pe.wait_ge(bank_free[t // 2], 2 * pair + unit + 1)
                    for k in range(KT):
                        for n, (w, a) in enumerate(((w_hi, h_hi), (w_lo, h_hi), (w_hi, h_lo))):
                            last = pe.matmul(
                                proj[:, t // 2, UNIT * (t % 2):UNIT * (t % 2 + 1)].rearrange("p (a n) -> p a n", a=2),
                                a[:, k, t * P:(t + 1) * P], w[:, slot:slot + 2, k, :],
                                start=k == 0 and n == 0, stop=k == KT - 1 and n == 2)
                last.then_inc(proj_done, 2)

            def mean_square(n):
                pe.wait_ge(sq_summed, n + 1)
                pe.matmul(att[:, 0, :], ones[:, :], sq_sum, start=True, stop=True).then_inc(ms_done, 1)

            def normed_ready(n):
                return lambda k: pe.wait_ge(h_ready, KT * n + k + 1)

            with pe.Fori(0, DEPTH) as layer:
                first = layer * LAYER_PAIRS
                mean_square(2 * layer)

                with pe.Fori(0, RET_LOOPS) as i:
                    pair = first + RET_PAIRS * i
                    for h in range(2):
                        head = 4 * layer + 2 * i + h
                        u = 6 * h
                        whole_unit(pair, u, h_hi, h_lo, normed_ready(2 * layer) if h == 0 else None)
                        whole_unit(pair, u + 1, h_hi, h_lo)
                        token_unit(pair, u + 2)
                        token_unit(pair, u + 3)
                        pe.wait_ge(qk_rotated, 2 * head + 2)
                        for j in range(TB):
                            for half in range(2):
                                last = pe.matmul(att_flat[:, OFF[j]:OFF[j] + WID[j]],
                                                 qk[:, 2 + half, P * j:P * (j + 1)], qk[:, half, P * j:SEQ],
                                                 start=half == 0, stop=half == 1)
                        last.then_inc(scores_done, 1)
                        half_unit(pair, u + 4, 0, h_hi, h_lo)
                        half_unit(pair, u + 4, 1, h_hi, h_lo)
                        pe.wait_ge(probs_ready, head + 1)
                        pe.wait_ge(bank_free[1], 2 * pair + u + 5)
                        for t in range(TB):
                            if t == 2:
                                half_unit(pair, u + 5, 0, h_hi, h_lo)
                            for j in range(t + 1):
                                at = OFF[j] + P * (t - j)
                                last = pe.matmul(att[:, RET_BANKS[t], :], p_ret[:, at:at + P], v_ret[:, j, :],
                                                 start=j == 0, stop=j == t)
                            last.then_inc(ret_done, 1)
                        half_unit(pair, u + 5, 1, h_hi, h_lo)
                        for t in range(TB):
                            pe.wait_ge(ret_normed, 4 * head + t + 1)
                            if t >= 2:
                                pe.wait_ge(ret_gated, 4 * head + t - 1)
                            for e in range(4):
                                last = pe.transpose(att[:, t % 2, P * e:P * (e + 1)], qk[:, t, P * e:P * (e + 1)],
                                                    ident[:, :])
                            last.then_inc(ret_turned, 1)

                    def gated_ready(k):
                        if k % 4 == 0:
                            pe.wait_ge(ret_gated, 4 * (4 * layer + 2 * i + k // 4) + 4)

                    for m in range(4):
                        whole_unit(pair, 12 + m, y_hi, y_lo, gated_ready if m == 0 else None)

                def scores(n, tile):
                    for j in range(TB):
                        if j == 2:
                            pe.wait_ge(sb_ready, n + 1)
                        for a in range(2):
                            r = slice(SB_DIM * a, SB_DIM * (a + 1))
                            at = 3 * a * SEQ + OFF[j]
                            last = pe.matmul(att_flat[:, at:at + WID[j]],
                                             tile2(sb_now, now_k)[r, tile, P * j:P * (j + 1)],
                                             tile2(sb_now, now_q)[r, tile, P * j:SEQ],
                                             start=j < 3, stop=True, skip_group_check=True)
                            if j == 3:
                                last.then_inc(z_done, 1)

                def break_stick(n):
                    for a in range(2):
                        pe.wait_ge(sp_ready, 2 * n + a + 1)
                        for i in range(TB):
                            for j in range(i, TB):
                                at = 3 * a * SEQ + OFF[i] + P * (j - i)
                                for sp_part in (sp_hi, sp_lo):
                                    last = pe.matmul(att_flat[:, at:at + WID[j]],
                                                     (neg_tri if i == j else neg_ones)[:, :],
                                                     sp_part[:, a, OFF[j]:OFF[j] + WID[j]],
                                                     start=False, stop=True, skip_group_check=True)
                        last.then_inc(broken, 1)

                def outputs(n, tile):
                    pe.wait_ge(weights_ready, 2 * n + 2)
                    for j in range(TB):
                        for a in range(2):
                            col = 2 * SB_DIM * tile + SB_DIM * a
                            last = pe.matmul(att[SB_DIM * a:SB_DIM * (a + 1), SB_OUT_BANK, P * j:SEQ],
                                             blocks(sb_now, now_v)[:, j, col:col + SB_DIM],
                                             terms[:, a, OFF[j]:OFF[j] + WID[j]],
                                             start=j == 0, stop=j == TB - 1, skip_group_check=True)
                    last.then_inc(sb_done, 1)

                whole_unit(first, SB_FIRST, h_hi, h_lo)
                token_unit(first, SB_FIRST + 1)
                whole_unit(first, SB_FIRST + 2, h_hi, h_lo)

                def group(pair, g, at, last):
                    n = 8 * layer + 2 * g
                    pe.wait_ge(qk_now, SB_GROUPS * layer + g + 1)
                    scores(n, 0)
                    whole_unit(pair, at, h_hi, h_lo)
                    half_unit(pair, at + 1, 0, h_hi, h_lo)
                    break_stick(n)
                    half_unit(pair, at + 1, 1, h_hi, h_lo)
                    pe.wait_ge(v_now, SB_GROUPS * layer + g + 1)
                    outputs(n, 0)
                    scores(n + 1, 1)
                    if last:
                        whole_unit(pair, at + 2, h_hi, h_lo)
                    else:
                        token_unit(pair, at + 2)
                    half_unit(pair, at + 3, 0, h_hi, h_lo)
                    break_stick(n + 1)
                    half_unit(pair, at + 3, 1, h_hi, h_lo)
                    outputs(n + 1, 1)

                with pe.Fori(0, SB_GROUPS - 1) as g:
                    group(first + 2 * g, g, SB_LOOP, False)
                group(first, SB_GROUPS - 1, SB_LAST, True)

                whole_unit(first, GB_LAST, h_hi, h_lo)
                for m in range(4):
                    whole_unit(first, SB_OUT + m, y_hi, y_lo,
                               (lambda k: pe.wait_ge(sb_ready, 8 * layer + k + 2)) if m == 0 else None)
                for m in range(4):
                    whole_unit(first, MIX + m, h_hi, h_lo,
                               (lambda k: pe.wait_ge(merged_ready, KT * layer + k + 1)) if m == 0 else None)
                mean_square(2 * layer + 1)
                with pe.Fori(0, QUARTERS) as f:
                    pair = first + 4 * f
                    for m in range(4):
                        whole_unit(pair, MLP + m, h_hi, h_lo, normed_ready(2 * layer + 1) if m == 0 else None)
                    for m in range(4):
                        whole_unit(pair, MLP + 4 + m, y_hi, y_lo,
                                   (lambda k: pe.wait_ge(u_split, KT * (4 * layer + f) + k + 1)) if m == 0 else None)

            mean_square(2 * DEPTH)
            for t in range(TB):
                for half in range(2):
                    bank = 2 * (t % 3) + half
                    if t == 3:
                        pe.wait_ge(y_stored if half else y_stored_dve, 1)
                    for k in range(4 * half, 4 * half + 4):
                        pe.wait_ge(y_normed, k + 1)
                        last = pe.transpose(att[:, bank, P * (k % 4):P * (k % 4 + 1)], y_T[:, k, P * t:P * (t + 1)],
                                            ident[:, :])
                    last.then_inc(y_turned, 1)

        @block.vector
        def _(dve):
            own = Chain(dve, dve_own)
            own.mark(dve.memset(eps_c[:, :], EPS))
            own.mark(dve.memset(gn_eps_c[:, :], GN_EPS))
            for s in range(2):
                dve.sem_inc(bank_free[s], 1)
            dve.sem_inc(gate_used, 1)
            dve.sem_inc(sb_ready, 1)
            n_rows = DEPTH * MODS * KT
            dve.wait_ge(vecs_turned, 1)
            own.link(dve.tensor_copy(mod[:, :], att[:, 0, 0:n_rows]))
            dve.tensor_copy(vecs[:, :, :], att[:, 0, n_rows:n_rows + 6 * KT].rearrange("p (a b) -> p a b", a=6)
                            ).then_inc(vecs_ready, 1)
            dve.wait_ge(vecs_ready, 1)
            dve.wait_ge(c_sig, 1)
            dve.tensor_tensor(c_act[:, :], c_act[:, :], vecs[:, 0, :], ALU.mult).then_inc(c_ready, 1)
            for k in range(0, KT, 2):
                dve.wait_ge(x_turned, k + 1)
                dve.tensor_copy(x_T[:, k, :], att[:, k % 6, :]).then_inc(x_ready_dve, 1)
            dve.wait_ge(ada_done, DEPTH * MODS * D // UNIT + 2)
            own.link(dve.tensor_tensor(mod[:, :], mod[:, :], proj[:, 0, 0:n_rows], ALU.add))
            for layer in range(DEPTH):
                for which, shift, scale in ((0, SHIFT1, SCALE1), (1, SHIFT2, SCALE2)):
                    n = 2 * layer + which
                    at = layer * MODS * KT
                    own.mark(dve.scalar_tensor_tensor(
                        n_scale[:, KT * n:KT * (n + 1)], mod[:, at + KT * scale:at + KT * (scale + 1)], 1.0,
                        vecs[:, 1 + 2 * which + layer, :], ALU.add, ALU.mult))
                    own.link(dve.tensor_copy(n_shift[:, KT * n:KT * (n + 1)],
                                             mod[:, at + KT * shift:at + KT * (shift + 1)]))
            own.settle()
            dve.sem_inc(mods_ready, 1)

            def products(pair, unit, half):
                dve.wait_ge(proj_done, 4 * pair + 2 * unit + half + 1)

            def taken(pair, unit, half):
                dve.wait_ge(bank_free[half], 2 * pair + unit + 2)

            def free(ins, half):
                ins.then_inc(bank_free[half], 1)

            def norm(n, dst, ring):
                for k in range(1, KT):
                    dve.wait_ge(squared, KT * n + k + 1)
                    if k >= 2:
                        dve.wait_ge(sq_used, 7 * n + k)
                    a = sq[:, 0, :] if k == 1 else sq_sum
                    ins = dve.tensor_tensor(sq_sum, a, sq[:, k % 2, :], ALU.add)
                    if k == KT - 1:
                        ins.then_inc(sq_summed, 1)
                    else:
                        ins.then_inc(sq_used, 2 if k == 1 else 1)
                dve.wait_ge(rstd_ready, n + 1)
                for k in range(KT + 1):
                    if k < KT:
                        if ring == 2 and k >= 2:
                            dve.wait_ge(h_ready, KT * n + k - 1)
                        dve.tensor_tensor(dst[:, k % ring, :], x_T[:, k, :], rstd, ALU.mult).then_inc(x_normed, 1)
                    if ring == 2 and k >= 1:
                        dve.wait_ge(h_half, KT * n + k)
                        dve.tensor_tensor(h_lo[:, k - 1, :], normed[:, (k - 1) % 2, :], h_hi[:, k - 1, :],
                                          ALU.subtract).then_inc(h_ready, 1)

            def add_to_x(pair, unit, half, k, gate_col):
                products(pair, unit, half)
                free(dve.scalar_tensor_tensor(x_T[:, k, :], proj[:, half, :], mod[:, ds(gate_col + k, 1)],
                                              x_T[:, k, :], ALU.mult, ALU.add), half)

            with own.loop(DEPTH, 132) as layer:
                first = layer * LAYER_PAIRS
                dve.wait_ge(x_turned, KT)
                dve.memset(ya[:, :, :], 0.0)
                norm(2 * layer, normed, 2)
                with own.loop(RET_LOOPS, 42) as i:
                    pair = first + RET_PAIRS * i
                    for h in range(2):
                        head = 4 * layer + 2 * i + h
                        u = 6 * h
                        dve.wait_ge(rope_in, 16 * layer + 16)
                        for n in range(2):
                            a, b = qk[:, 2 * n, :], qk[:, 2 * n + 1, :]
                            products(pair, u + n, 0)
                            dve.tensor_tensor(a, proj[:, 0, :], rope_t[:, 0, :], ALU.mult)
                            free(dve.tensor_tensor(b, proj[:, 0, :], rope_t[:, 1, :], ALU.mult), 0)
                            products(pair, u + n, 1)
                            own.link(dve.tensor_tensor(rot, proj[:, 1, :], rope_t[:, 1, :], ALU.mult))
                            own.link(dve.tensor_tensor(a, a, rot, ALU.subtract))
                            free(dve.tensor_tensor(rot, proj[:, 1, :], rope_t[:, 0, :], ALU.mult), 1)
                            dve.wait_ge(bank_free[1], 2 * pair + u + n + 2)
                            dve.tensor_tensor(b, b, rot, ALU.add).then_inc(qk_rotated, 1)
                            dve.wait_ge(qk_rotated, 2 * head + n + 1)
                        dve.wait_ge(decay_in, 16 * head + 16)
                        dve.wait_ge(scores_done, head + 1)
                        for j in (0, 1, 3, 2):
                            ins = dve.tensor_tensor(p_ret[:, OFF[j]:OFF[j] + WID[j]], att_flat[:, OFF[j]:OFF[j] + WID[j]],
                                                    decay_t[:, 0:WID[j]], ALU.mult)
                        ins.then_inc(probs_ready, 1)

                        def silu(n):
                            dve.wait_ge(sig_ready, 4 * head + n + 1)
                            free(dve.tensor_tensor(g_ret[:, n, :], g_ret[:, n, :], proj[:, n % 2, :], ALU.mult), n % 2)

                        def moments_of(t):
                            dve.wait_ge(ret_done, 4 * head + t + 1)
                            own.mark(dve.bn_stats(stats[:, t, :], att[:, RET_BANKS[t], :]))

                        silu(0)
                        silu(1)
                        moments_of(0)
                        moments_of(1)
                        silu(2)
                        moments_of(2)
                        moments_of(3)
                        own.settle()
                        own.mark(dve.tensor_tensor(mean_diff[:, :], stats[:, :, 1], stats[:, :, 4], ALU.subtract))
                        own.mark(dve.tensor_tensor(moments[:, :, 0], stats[:, :, 1], stats[:, :, 4], ALU.add))
                        own.link(dve.tensor_tensor(moments[:, :, 1], stats[:, :, 2], stats[:, :, 5], ALU.add))
                        own.link(dve.scalar_tensor_tensor(mean_diff[:, :], mean_diff[:, :], RET_V / 4.0,
                                                          mean_diff[:, :], ALU.mult, ALU.mult))
                        own.link(dve.tensor_scalar(moments[:, :, 0], moments[:, :, 0], 0.5, None, ALU.mult))
                        dve.tensor_tensor(moments[:, :, 1], moments[:, :, 1], mean_diff[:, :],
                                          ALU.add).then_inc(moments_ready, 1)
                        dve.wait_ge(ret_rstd_ready, head + 1)
                        for t in range(TB):
                            dve.tensor_scalar(qk[:, t, :], att[:, RET_BANKS[t], :], moments[:, t, 0:1],
                                              ret_rstd[:, t:t + 1], ALU.subtract, ALU.mult).then_inc(ret_normed, 1)
                        silu(3)
                        taken(pair, u + 5, 1)
                        for t in range(TB):
                            dve.wait_ge(ret_turned, 4 * head + t + 1)
                            gated = gated_t.rearrange("p (e t) -> p e t", e=4)
                            tok = slice(P * t, P * (t + 1))
                            e4 = slice(4 * h, 4 * h + 4)
                            own.link(dve.tensor_tensor(gated, g_ret[:, :, tok],
                                                       att[:, t % 2, :].rearrange("p (e t) -> p e t", e=4), ALU.mult))
                            own.link(dve.tensor_copy(y_hi[:, e4, tok], gated))
                            dve.tensor_tensor(y_lo[:, e4, tok], gated, y_hi[:, e4, tok],
                                              ALU.subtract).then_inc(ret_gated, 1)
                            dve.wait_ge(ret_gated, 4 * head + t + 1)
                    for m in range(4):
                        for half in range(2):
                            products(pair, 12 + m, half)
                            k = 2 * m + half
                            free(dve.tensor_tensor(ya[:, k, :], ya[:, k, :], proj[:, half, :], ALU.add), half)

                def mask(buf):
                    three = buf[:, 0:3 * SEQ - 2 * P].rearrange("p (j n) -> p j n", n=P)[:, 0:9:4, :]
                    dve.tensor_tensor(three, three, upto[:, :].rearrange("p (a n) -> p a n", a=1).to_broadcast([P, 3, P]),
                                      ALU.min)
                    one = buf[:, OFF[3]:OFF[3] + P]
                    return dve.tensor_tensor(one, one, upto[:, :], ALU.min)

                def softplus(n):
                    for a in range(2):
                        dve.wait_ge(log_ready, 2 * n + a + 1)
                        own.link(dve.scalar_tensor_tensor(terms[:, a, :], scores_of(a), 0.0, terms[:, a, :],
                                                          ALU.max, ALU.add))
                        own.link(mask(terms[:, a, :]))
                        own.link(dve.tensor_copy(sp_hi[:, a, :], terms[:, a, :]))
                        dve.tensor_tensor(sp_lo[:, a, :], terms[:, a, :], sp_hi[:, a, :],
                                          ALU.subtract).then_inc(sp_ready, 1)

                def mask_weights(n):
                    for a in range(2):
                        dve.wait_ge(weights_exp, 2 * n + a + 1)
                        mask(terms[:, a, :]).then_inc(weights_ready, 1)

                def low_output(n, tile):
                    dve.wait_ge(sb_half, n + 1)
                    dve.tensor_tensor(y_lo[:, tile, :], att[:, SB_OUT_BANK:SB_OUT_BANK + 1, :], y_hi[:, tile, :],
                                      ALU.subtract).then_inc(sb_ready, 1)

                def take_qk(pair, unit):
                    taken(pair, unit, 1)
                    for part_of in (now_k, now_q):
                        ins = dve.tensor_copy(sb_now[:, part_of, :], sb_next[:, part_of, :])
                    ins.then_inc(qk_now, 1)

                def take_v():
                    dve.tensor_copy(sb_now[:, now_v, :], sb_next[:, now_v, :]).then_inc(v_now, 1)

                take_qk(first, SB_FIRST + 2)
                take_v()

                def group(pair, g, at, last):
                    n = 8 * layer + 2 * g
                    softplus(n)
                    for half in range(2):
                        taken(pair, at, half)
                        dve.tensor_tensor(ya[:, ds(2 * g + half, 1), :], ya[:, ds(2 * g + half, 1), :],
                                          gate_t.rearrange("p (a n) -> p a n", a=1), ALU.mult).then_inc(gate_used, 1)
                    mask_weights(n)
                    low_output(n, ds(2 * g, 1))
                    softplus(n + 1)
                    mask_weights(n + 1)
                    if not last:
                        take_qk(pair, at + 3)
                    low_output(n + 1, ds(2 * g + 1, 1))
                    if not last:
                        take_v()

                with own.loop(SB_GROUPS - 1, 12) as g:
                    group(first + 2 * g, g, SB_LOOP, False)
                group(first, SB_GROUPS - 1, SB_LAST, True)

                for m in range(4):
                    for half in range(2):
                        k = 2 * m + half
                        products(first, SB_OUT + m, half)
                        free(dve.tensor_tensor(merged_t[:, half, :], proj[:, half, :], sg[:, k, :], ALU.mult), half)
                        dve.wait_ge(bank_free[half], 2 * first + SB_OUT + m + 2)
                        dve.tensor_tensor(merged_t[:, half, :], merged_t[:, half, :], ya[:, k, :],
                                          ALU.add).then_inc(merged_sum, 1)
                        dve.wait_ge(merged_half, KT * layer + k + 1)
                        dve.tensor_tensor(h_lo[:, k, :], merged_t[:, half, :], h_hi[:, k, :],
                                          ALU.subtract).then_inc(merged_ready, 1)
                gates = MODS * KT * layer
                for m in range(4):
                    for half in range(2):
                        add_to_x(first, MIX + m, half, 2 * m + half, gates + KT * GATE1)
                norm(2 * layer + 1, normed, 2)

                with own.loop(QUARTERS, 0) as f:
                    pair = first + 4 * f
                    for m in range(4):
                        for half in range(2):
                            k = 2 * m + half
                            n = KT * (4 * layer + f) + k
                            taken(pair, MLP + m, half)
                            dve.tensor_tensor(u_t[:, half, :], relu_t[:, half, :], relu_t[:, half, :],
                                              ALU.mult).then_inc(u_ready, 1)
                            dve.wait_ge(u_half, n + 1)
                            dve.tensor_tensor(y_lo[:, k, :], u_t[:, half, :], y_hi[:, k, :],
                                              ALU.subtract).then_inc(u_split, 1)
                    for m in range(4):
                        for half in range(2):
                            add_to_x(pair, MLP + 4 + m, half, 2 * m + half, gates + KT * GATE2)

            norm(2 * DEPTH, y_T, KT)
            for t in range(TB):
                dve.wait_ge(y_turned, 2 * t + 1)
                dve.tensor_copy(x_tok[:, t, 0:SEQ], att[:, 2 * (t % 3), :]).then_inc(y_stored_dve, 1)


def rope_tables():
    half = RET_QK // 2
    inv_freq = np.power(np.float32(10000.0), -np.arange(half, dtype=np.float32) / np.float32(half))
    angle = inv_freq[:, None] * np.arange(SEQ, dtype=np.float32)[None, :]
    return np.stack([np.cos(angle), np.sin(angle)], axis=1).astype(np.float32)


def decay_tables():
    gamma = 1.0 - 2.0 ** (-5.0 - np.arange(RET_HEADS))
    rel = np.arange(SEQ)[None, None, :] - np.arange(P)[:, None, None]
    table = np.where(rel >= 0, gamma[None, :, None] ** np.maximum(rel, 0), 0.0) * RET_QK ** -0.5
    return table.astype(np.float32)


_INS = ["x", "c", "norm_mix_g", "w_in", "w_ret_out", "w_sb_out", "w_mix_out", "norm_mlp_g",
        "w_up", "w_down", "w_ada", "b_ada", "final_g"]


def kernel(**inputs):
    import concourse.bacc as bacc
    from concourse.bass_utils import run_bass_kernel_spmd

    nc = bacc.Bacc("TRN2", target_bir_lowering=False, num_devices=1)
    arrays = {name: np.ascontiguousarray(inputs[name]) for name in _INS}
    arrays["rope"] = rope_tables()
    arrays["decay"] = decay_tables()
    args = [nc.dram_tensor(f"in_{name}", a.shape, mybir.dt.from_np(a.dtype), kind="ExternalInput").ap()
            for name, a in arrays.items()]
    out = nc.dram_tensor("out", inputs["x"].shape, mybir.dt.float32, kind="ExternalOutput").ap()
    hybrid_trunk(nc, *args, out)
    result = run_bass_kernel_spmd(nc, [{f"in_{name}": a for name, a in arrays.items()}], core_ids=[0])
    return result.results[0]["out"]
```

```python
import math
from contextlib import ExitStack, contextmanager

import numpy as np

import concourse.bass as bass
from concourse import mybir

P = 128
D = 1024
SEQ = 512
DEPTH = 2
KT = D // P
TB = SEQ // P
UNIT = 256
IN_W = 11264
RET_HEADS, RET_QK, RET_V = 4, 256, 512
SB_HEADS, SB_DIM = 16, 64
SB_GROUPS = SB_HEADS * SB_DIM // UNIT
D_FF = 4096
QUARTERS = D_FF // D
MODS = 6
SHIFT1, SCALE1, GATE1, SHIFT2, SCALE2, GATE2 = range(MODS)
EPS, GN_EPS = 1e-6, 1e-5
RQ, RK, RV, RG = 0, 1024, 2048, 4096
SQ, SK, SV, GA, GB = 6144, 7168, 8192, 9216, 10240

RET_LOOPS = RET_HEADS // 2
RET_PAIRS = 8
SB_FIRST = RET_LOOPS * RET_PAIRS * 2
SB_LOOP = SB_FIRST + 3
SB_LAST = SB_LOOP + 4 * (SB_GROUPS - 1)
GB_LAST = SB_LAST + 4
SB_OUT = GB_LAST + 1
MIX = SB_OUT + 4
MLP = MIX + 4
LAYER_UNITS = MLP + 8 * QUARTERS
LAYER_PAIRS = LAYER_UNITS // 2
UNITS = DEPTH * LAYER_UNITS
ADA_FIRST = 2 * D // UNIT
FIRST_ON_PE = list(range(1, ADA_FIRST, 3))
FIRST_ON_DVE = [n for n in range(ADA_FIRST) if n not in FIRST_ON_PE]
ADA_UNITS = MODS * D // UNIT
ADA_SUMS = [[0, 1], [2, 3], [4, 5], [None, 6], [7, 8], [9, 10], [11], []]
ADA_LOADS = [[]] + ADA_SUMS[:-1]
LO_CREDIT = 4

OFF = [0, 512, 1024, 896]
WID = [SEQ - P * j for j in range(TB)]
CAUSAL = sum(WID)
BY_TILE = (1, 1, 1, 1, 1, 3)
BIG = 3.0e38


def ada_of(m, half):
    return ADA_SUMS[m][half] if half < len(ADA_SUMS[m]) else None


class Chain:

    def __init__(self, eng, sem):
        self.eng, self.sem, self.base, self.count = eng, sem, 0, 0

    def mark(self, ins):
        ins.then_inc(self.sem, 1)
        self.count += 1

    def settle(self):
        self.eng.wait_ge(self.sem, self.base + self.count)

    def link(self, ins):
        self.mark(ins)
        self.settle()

    @contextmanager
    def loop(self, times, per):
        base, before = self.base, self.count
        with self.eng.Fori(0, times) as i:
            self.base, self.count = base + before + per * i, 0
            yield i
            assert self.count == per, f"the loop marks {self.count} times, not {per}"
        self.base, self.count = base, before + per * times


def hybrid_trunk(nc, x, c, norm_mix_g, w_in, w_ret_out, w_sb_out, w_mix_out, norm_mlp_g,
                 w_up, w_down, w_ada, b_ada, final_g, rope, decay, out):
    f32, f32r = mybir.dt.float32, mybir.dt.float32r
    ALU, ACT = mybir.AluOpType, mybir.ActivationFunctionType
    ds = bass.ds
    EXP_LN = "natural_log_exp_and_others"

    ctx = ExitStack()
    with ctx:
        def sb(name, shape, dt=f32):
            return ctx.enter_context(nc.sbuf_tensor(name, shape, dt))

        def sem(name):
            return ctx.enter_context(nc.semaphore(name))

        x_T = sb("x_T", [P, KT, SEQ])
        h_hi = sb("h_hi", [P, KT, SEQ], f32r)
        h_lo = sb("h_lo", [P, KT, SEQ], f32r)
        y_hi = sb("y_hi", [P, KT, SEQ], f32r)
        y_lo = sb("y_lo", [P, KT, SEQ], f32r)
        ya = sb("ya", [P, KT, SEQ])
        w_raw = sb("w_raw", [P, 2, KT, UNIT])
        w_hi = sb("w_hi", [P, 4, KT, P], f32r)
        w_lo = sb("w_lo", [P, 4, KT, P], f32r)
        sp_hi = sb("sp_hi", [P, 2, CAUSAL], f32r)
        sp_lo = sb("sp_lo", [P, 2, CAUSAL], f32r)
        ident = sb("ident", [P, P])
        ones = sb("ones", [P, P])
        upto = sb("upto", [P, P])
        neg_tri = sb("neg_tri", [P, P], f32r)
        neg_ones = sb("neg_ones", [P, P], f32r)
        mod = sb("mod", [P, (DEPTH * MODS + 2) * KT])
        vecs = sb("vecs", [P, 6, KT])
        c_act = sb("c_act", [P, KT])
        ada_sum = sb("ada_sum", [P, 2, UNIT])
        one_c = sb("one_c", [P, 1])
        n_scale = sb("n_scale", [P, 2 * DEPTH * KT])
        n_shift = sb("n_shift", [P, 2 * DEPTH * KT])
        eps_c = sb("eps_c", [P, 1])
        gn_eps_c = sb("gn_eps_c", [P, 1])
        WORK = 9216
        work = sb("work", [P, WORK])

        def part(at, *shape):
            n = math.prod(shape)
            assert at + n <= WORK
            v = work[:, at:at + n]
            if len(shape) == 2:
                v = v.rearrange("p (a b) -> p a b", a=shape[0])
            if len(shape) == 3:
                v = v.rearrange("p (a b c) -> p a b c", a=shape[0], b=shape[1])
            return v

        ada_first = part(0, 3, KT, UNIT)
        rows = part(8192, P)
        neg_f = part(8320, P)
        ada_raw = part(5120, 2, KT, UNIT)
        x_tok = ya[:, :, :].rearrange("p a b -> p (a b)").rearrange("p (t d) -> p t d", t=TB)
        at_layer = (part(6144, 2, SEQ), part(7168, SEQ), part(7680, SEQ), part(0, 2, SEQ))
        at_mlp = (part(0, 2, SEQ), part(1024, SEQ), part(1536, SEQ), part(2048, 2, SEQ))
        qk = part(0, 4, SEQ)
        v_ret = part(2048, TB, RET_V)
        g_ret = part(4096, TB, SEQ)
        p_ret = part(6144, CAUSAL)
        rope_t = part(7424, 2, SEQ)
        rot = part(8448, SEQ)
        gated_t = rot
        stats = sb("stats", [P, TB, 6])
        moments = sb("moments", [P, TB, 2])
        mean_diff = sb("mean_diff", [P, TB])
        ret_rstd = sb("ret_rstd", [P, TB])
        decay_t = sb("decay_t", [P, SEQ])
        sb_next = part(0, 3, 1024)
        sb_now = part(3072, 3, 1024)
        terms = part(6144, 2, CAUSAL)
        gate_t = part(8704, SEQ)
        sg = part(0, KT, SEQ)
        merged_t = part(4096, 2, SEQ)
        relu_t = part(0, 2, SEQ)
        u_t = part(1024, 2, SEQ)
        y_T = part(3072, KT, SEQ)

        now_k, now_v, now_q = 0, 1, 2

        def tile2(buf, i):
            return buf[:, i, :].rearrange("p (a t) -> p a t", a=2)

        def blocks(buf, i):
            return buf[:, i, :].rearrange("p (s d) -> p s d", s=TB)

        proj = ctx.enter_context(nc.psum_tensor("proj", [P, 2, SEQ], f32))
        att = ctx.enter_context(nc.psum_tensor("att", [P, 6, SEQ], f32))
        att_flat = att[:, :, :].rearrange("p b n -> p (b n)")

        RET_BANKS = [3, 4, 5, 2]
        TURNED_BANKS = [0, 1, 3, 4]
        SB_OUT_BANK = 5

        def first_sum(d):
            d = d % 4
            return ada_sum[:, d, :] if d < 2 else decay_t[:, (d - 2) * UNIT:(d - 1) * UNIT]

        def scores_of(a):
            return att_flat[:, 3 * a * SEQ:3 * a * SEQ + CAUSAL]

        rows_in, consts_in = sem("rows_in"), sem("consts_in")
        x_in, out_stored = sem("x_in"), sem("out_stored")
        first_in = [sem(f"first_in{s}") for s in range(3)]
        ada_in = [sem("ada_in0"), sem("ada_in1")]
        ada_summed, ada_turned = sem("ada_summed"), sem("ada_turned")
        first_summed, first_turned = sem("first_summed"), sem("first_turned")
        decay_in, rope_in = sem("decay_in"), sem("rope_in")
        raw_in = [sem("raw_in0"), sem("raw_in1")]
        consts_made, vecs_turned, vecs_ready = sem("consts_made"), sem("vecs_turned"), sem("vecs_ready")
        x_turned, x_ready, x_ready_dve = sem("x_turned"), sem("x_ready"), sem("x_ready_dve")
        c_sig, c_ready, ada_done, mods_ready = sem("c_sig"), sem("c_ready"), sem("ada_done"), sem("mods_ready")
        hi_ready, lo_ready = sem("hi_ready"), sem("lo_ready")
        proj_done = sem("proj_done")
        bank_free = [sem("bank_free0"), sem("bank_free1")]
        squared, sq_used, ms_done, rstd_ready = sem("squared"), sem("sq_used"), sem("ms_done"), sem("rstd_ready")
        x_normed, h_half, h_ready = sem("x_normed"), sem("h_half"), sem("h_ready")
        qk_rotated = sem("qk_rotated")
        scores_done, probs_ready, ret_done = sem("scores_done"), sem("probs_ready"), sem("ret_done")
        moments_ready, ret_rstd_ready, ret_normed = (
            sem("moments_ready"), sem("ret_rstd_ready"), sem("ret_normed"))
        ret_turned, ret_gated, sig_ready = sem("ret_turned"), sem("ret_gated"), sem("sig_ready")
        z_done, log_ready, sp_ready = sem("z_done"), sem("log_ready"), sem("sp_ready")
        broken, weights_exp, weights_ready = sem("broken"), sem("weights_exp"), sem("weights_ready")
        sb_done, sb_half, sb_ready = sem("sb_done"), sem("sb_half"), sem("sb_ready")
        qk_now, v_now = sem("qk_now"), sem("v_now")
        gate_used, merged_sum, merged_half, merged_ready = (
            sem("gate_used"), sem("merged_sum"), sem("merged_half"), sem("merged_ready"))
        u_ready, u_half, u_split = sem("u_ready"), sem("u_half"), sem("u_split")
        y_turned, y_stored, y_stored_dve = (
            sem("y_turned"), sem("y_stored"), sem("y_stored_dve"))
        dve_own, act_own = sem("dve_own"), sem("act_own")

        def tiles(w):
            return w.rearrange("l (k p) n -> p l k n", p=P)

        win_v, wret_v, wsb_v, wmix_v, wup_v, wdown_v, wada_v = map(
            tiles, (w_in, w_ret_out, w_sb_out, w_mix_out, w_up, w_down, w_ada))

        block = ctx.enter_context(nc.Block())

        @block.sync
        def _(sp):
            bias_rows = b_ada.rearrange("l (n p) -> (l n) p", p=P)
            sp.dma_start(rows[0:bias_rows.shape[0], :], bias_rows).then_inc(rows_in, 16)
            sp.dma_start(x_tok, x.rearrange("b (t p) d -> p (b t) d", p=P)).then_inc(x_in, 16)
            for n in range(ADA_FIRST):
                if n - 3 in FIRST_ON_PE:
                    sp.wait_ge(ada_done, FIRST_ON_PE.index(n - 3) + 1)
                elif n >= 3:
                    sp.wait_ge(first_summed, FIRST_ON_DVE.index(n - 3) + 1)
                sp.dma_start(ada_first[:, n % 3:n % 3 + 1, :, :],
                             wada_v[:, 0:1, :, n * UNIT:(n + 1) * UNIT]).then_inc(first_in[n % 3], 16)

            def load_ada(layer, n, src_layer, col):
                sp.wait_ge(ada_summed, ADA_UNITS * layer + n + 1)
                sp.dma_start(ada_raw[:, n % 2:n % 2 + 1, :, :],
                             wada_v[:, ds(src_layer, 1), :, ds(col, UNIT)]).then_inc(ada_in[n % 2], 16)

            def load(pair, unit, src):
                s = unit % 2
                sp.wait_ge(lo_ready, 4 * pair + 2 * unit - 2 + LO_CREDIT)
                sp.dma_start(w_raw[:, s:s + 1, :, :], src).then_inc(raw_in[s], 16)

            with sp.Fori(0, DEPTH) as layer:
                l1 = ds(layer, 1)
                first = layer * LAYER_PAIRS

                def w_in_cols(col):
                    return win_v[:, l1, :, ds(col, UNIT)]

                with sp.Fori(0, RET_LOOPS) as i:
                    pair = first + RET_PAIRS * i
                    for j in range(2):
                        head_qk, head_v = (2 * i + j) * RET_QK, (2 * i + j) * RET_V
                        cols = [RQ + head_qk, RK + head_qk, RV + head_v, RV + UNIT + head_v,
                                RG + head_v, RG + UNIT + head_v]
                        for n, col in enumerate(cols):
                            load(pair, 6 * j + n, w_in_cols(col))
                    for m in range(4):
                        load(pair, 12 + m, wret_v[:, l1, ds(KT * i, KT), m * UNIT:(m + 1) * UNIT])
                for n, col in enumerate([SK, SV, SQ]):
                    load(first, SB_FIRST + n, win_v[:, l1, :, col:col + UNIT])
                with sp.Fori(0, SB_GROUPS - 1) as g:
                    pair = first + 2 * g
                    for n, col in enumerate([GA - UNIT, SK, SV, SQ]):
                        load(pair, SB_LOOP + n, w_in_cols(g * UNIT + (col + UNIT)))
                for n, col in enumerate([GA + 3 * UNIT] + [GB + m * UNIT for m in range(4)]):
                    load(first, SB_LAST + n, win_v[:, l1, :, col:col + UNIT])
                for m in range(8):
                    load(first, SB_OUT + m, (wsb_v if m < 4 else wmix_v)[:, l1, :, m % 4 * UNIT:(m % 4 + 1) * UNIT])
                    if m == 1:
                        sp.wait_ge(sb_done, 8 * layer + 8)
                    for n in filter(lambda n: n is not None, ADA_LOADS[m]):
                        load_ada(layer, n, layer, ADA_FIRST * UNIT + n * UNIT)

                def load_quarter(pair, f, with_ada):
                    for m in range(4):
                        load(pair, MLP + m, wup_v[:, l1, :, ds(f * D + m * UNIT, UNIT)])
                        if with_ada:
                            sp.wait_ge(ada_summed, ADA_UNITS * layer + 4 * f + 12 + m + 1)
                            sp.dma_start(ada_raw[:, m % 2:m % 2 + 1, :, :],
                                         wada_v[:, ds((layer + (f + 1) // 2) % DEPTH, 1), :,
                                                ds((5 + f) % 6 * D + m * UNIT, UNIT)]).then_inc(ada_in[m % 2], 16)
                    for m in range(4):
                        load(pair, MLP + 4 + m, wdown_v[:, l1, ds(KT * f, KT), m * UNIT:(m + 1) * UNIT])

                with sp.Fori(0, QUARTERS - 1) as f:
                    load_quarter(first + 4 * f, f, True)
                load_quarter(first + 4 * (QUARTERS - 1), QUARTERS - 1, False)

            for t in range(TB):
                sp.wait_ge(y_stored, t + 1)
                sp.wait_ge(y_stored_dve, t + 1)
                sp.dma_start(out[0, t * P:(t + 1) * P, :], x_tok[:, t, :]).then_inc(out_stored, 16)
            sp.wait_ge(out_stored, 16 * TB)

        @block.gpsimd
        def _(pool):
            pool.memset(ident[:, :], 0.0).then_inc(consts_made, 1)
            pool.memset(ones[:, :], 1.0 / D).then_inc(consts_made, 1)
            pool.memset(upto[:, :], BIG).then_inc(consts_made, 1)
            pool.memset(neg_f, -1.0).then_inc(consts_made, 1)
            pool.memset(one_c[:, :], 1.0).then_inc(consts_made, 1)
            pool.wait_ge(consts_made, 5)
            pool.affine_select(out=ident[:, :], in_=ident[:, :], compare_op=ALU.not_equal, fill=1.0,
                               base=0, pattern=[[-1, P]], channel_multiplier=1).then_inc(consts_made, 1)
            pool.affine_select(out=upto[:, :], in_=upto[:, :], compare_op=ALU.is_gt, fill=0.0,
                               base=0, pattern=[[1, P]], channel_multiplier=-1).then_inc(consts_made, 1)
            pool.tensor_copy(neg_ones[:, :], neg_f).then_inc(consts_made, 1)
            pool.wait_ge(consts_made, 8)
            pool.affine_select(out=neg_f, in_=neg_f, compare_op=ALU.is_ge, fill=0.0,
                               base=0, pattern=[[-1, P]], channel_multiplier=1).then_inc(consts_made, 1)
            pool.wait_ge(consts_made, 9)
            pool.tensor_copy(neg_tri[:, :], neg_f).then_inc(consts_made, 1)
            pool.sem_inc(lo_ready, LO_CREDIT)
            with pool.Fori(0, UNITS // 2) as v:
                for s in range(4):
                    pool.wait_ge(hi_ready, 4 * v + s + 1)
                    pool.tensor_tensor(w_lo[:, s, :, :], w_raw[:, s // 2, :, P * (s % 2):P * (s % 2 + 1)],
                                       w_hi[:, s, :, :], ALU.subtract).then_inc(lo_ready, 1)

        @block.scalar
        def _(act):
            own = Chain(act, act_own)
            act.dma_start(decay_t[0:8, 0:P], c.rearrange("b (n p) -> (b n) p", p=P)).then_inc(consts_in, 16)
            act.dma_start(decay_t[8:24, 0:P], norm_mix_g.rearrange("l (n p) -> (l n) p", p=P)).then_inc(consts_in, 16)
            act.dma_start(decay_t[24:40, 0:P], norm_mlp_g.rearrange("l (n p) -> (l n) p", p=P)).then_inc(consts_in, 16)
            act.dma_start(decay_t[40:48, 0:P], final_g.rearrange("(n p) -> n p", p=P)).then_inc(consts_in, 16)
            act.wait_ge(vecs_ready, 1)
            act.activation(c_act[:, :], vecs[:, 0, :], ACT.Sigmoid).then_inc(c_sig, 1)
            act.preload_act_table_set(EXP_LN)

            def square(n, k, buffers):
                if k >= 2:
                    act.wait_ge(sq_used, 7 * n + max(2, k - 1))
                act.activation(buffers[0][:, k % 2, :], x_T[:, k, :], ACT.Square).then_inc(squared, 1)

            for k in range(KT):
                if k % 2:
                    act.wait_ge(x_turned, k + 1)
                    act.activation(x_T[:, k, :], att[:, k % 6, :], ACT.Copy).then_inc(x_ready, 1)
                    act.wait_ge(x_ready, k // 2 + 1)
                else:
                    act.wait_ge(x_ready_dve, k // 2 + 1)
                square(0, k, at_layer)

            def split_weights(pair, unit, j):
                s = unit % 2
                act.wait_ge(raw_in[s], 16 * (pair + unit // 2 + 1))
                act.activation(w_hi[:, 2 * s + j, :, :], w_raw[:, s, :, P * j:P * (j + 1)],
                               ACT.Copy).then_inc(hi_ready, 1)

            def products(pair, unit, j):
                act.wait_ge(proj_done, 4 * pair + 2 * unit + j + 1)

            def norm(n, buffers):
                rstd = buffers[2]
                act.wait_ge(ms_done, n + 1)
                own.link(act.activation(rstd, att[:, 0, :], ACT.Ln, bias=eps_c[:, :]))
                act.activation(rstd, rstd, ACT.Exp, scale=-0.5).then_inc(rstd_ready, 1)

            def norm_affine(n, buffers, between=None):
                norm(n, buffers)
                act.wait_ge(mods_ready, n + 1)
                normed = buffers[3]
                for k in range(KT):
                    act.wait_ge(x_normed, KT * n + k + 1)
                    act.activation(h_hi[:, k, :], normed[:, k % 2, :], ACT.Identity,
                                   bias=n_shift[:, ds(KT * n + k, 1)]).then_inc(h_half, 1)
                    if between and k % 2:
                        between(k // 2)

            def sigmoid(dst, src):
                ins = act.activation(dst, src, ACT.Sigmoid)
                act.preload_act_table_set(EXP_LN)
                return ins

            with own.loop(DEPTH, 38) as layer:
                first = layer * LAYER_PAIRS
                for j in range(2):
                    split_weights(first, 0, j)
                norm_affine(2 * layer, at_layer, lambda j: split_weights(first, 1, j) if j < 2 else None)
                act.dma_start(rope_t, rope).then_inc(rope_in, 16)

                with own.loop(RET_LOOPS, 2) as i:
                    pair = first + RET_PAIRS * i
                    for j in range(2):
                        head = 4 * layer + 2 * i + j
                        u = 6 * j
                        for unit in (u, u + 1):
                            for half in range(2):
                                products(pair, unit, half)
                                if unit == u and half == 0:
                                    act.dma_start(decay_t[:, :], decay[:, ds(2 * i + j, 1), :].rearrange("p a n -> p (a n)")
                                                  ).then_inc(decay_in, 16)
                                split_weights(pair, unit + 2, half)
                        for unit in (u + 2, u + 3):
                            for half in range(2):
                                products(pair, unit, half)
                                col = UNIT * (unit - u - 2)
                                act.activation(v_ret[:, 2 * half:2 * half + 2, col:col + UNIT],
                                               proj[:, half, :].rearrange("p (a n) -> p a n", a=2),
                                               ACT.Copy).then_inc(bank_free[half], 1)
                            for half in range(2):
                                split_weights(pair, unit + 2, half)
                        for n in range(4):
                            if n == 2:
                                act.preload_act_table_set(EXP_LN)
                                act.wait_ge(moments_ready, head + 1)
                                own.link(act.activation(ret_rstd[:, :], moments[:, :, 1], ACT.Ln, bias=gn_eps_c[:, :],
                                                        scale=1.0 / RET_V))
                                act.activation(ret_rstd[:, :], ret_rstd[:, :], ACT.Exp,
                                               scale=-0.5).then_inc(ret_rstd_ready, 1)
                            unit, half = u + 4 + n // 2, n % 2
                            products(pair, unit, half)
                            act.activation(g_ret[:, n, :], proj[:, half, :], ACT.Sigmoid).then_inc(sig_ready, 1)
                            split_weights(pair, unit + 2, half)
                        act.preload_act_table_set(EXP_LN)
                    for unit in range(12, 16):
                        for half in range(2):
                            products(pair, unit, half)
                            split_weights(pair, unit + 2, half)

                def store_feature(pair, unit, half, dst, scale=1.0):
                    products(pair, unit, half)
                    act.activation(dst, proj[:, half, :], ACT.Copy, scale=scale).then_inc(bank_free[half], 1)
                    split_weights(pair, unit + 2, half)

                def store_k(pair, unit, half):
                    store_feature(pair, unit, half, tile2(sb_next, now_k)[:, half, :])

                def store_q(pair, unit, half):
                    store_feature(pair, unit, half, tile2(sb_next, now_q)[:, half, :], SB_DIM ** -0.5)

                def store_v(pair, unit):
                    for half in range(2):
                        products(pair, unit, half)
                        act.activation(blocks(sb_next, now_v)[:, 2 * half:2 * half + 2, :],
                                       proj[:, half, :].rearrange("p (a n) -> p a n", a=2),
                                       ACT.Copy).then_inc(bank_free[half], 1)
                    for half in range(2):
                        split_weights(pair, unit + 2, half)

                def gate(pair, unit, half, dst, done):
                    products(pair, unit, half)
                    sigmoid(dst, proj[:, half, :]).then_inc(done, 1)
                    split_weights(pair, unit + 2, half)

                def logs(n):
                    for a in range(2):
                        act.wait_ge(z_done, 2 * n + a + 1)
                        own.link(act.activation(terms[:, a, :], scores_of(a), ACT.Abs))
                        own.link(act.activation(terms[:, a, :], terms[:, a, :], ACT.Exp, scale=-1.0))
                        act.activation(terms[:, a, :], terms[:, a, :], ACT.Ln, bias=1.0).then_inc(log_ready, 1)

                def weights(n):
                    for a in range(2):
                        act.wait_ge(broken, 2 * n + a + 1)
                        act.wait_ge(sp_ready, 2 * n + a + 1)
                        act.activation(terms[:, a, :], scores_of(a), ACT.Exp).then_inc(weights_exp, 1)

                def head_pair_out(n, tile):
                    act.wait_ge(sb_done, n + 1)
                    act.activation(y_hi[:, tile, :], att[:, SB_OUT_BANK:SB_OUT_BANK + 1, :], ACT.Copy).then_inc(sb_half, 1)

                for half in range(2):
                    store_k(first, SB_FIRST, half)
                store_v(first, SB_FIRST + 1)
                for half in range(2):
                    store_q(first, SB_FIRST + 2, half)

                def group(pair, g, at, last):
                    n = 8 * layer + 2 * g
                    logs(n)
                    for half in range(2):
                        act.wait_ge(gate_used, 8 * layer + 2 * g + half + 1)
                        products(pair, at, half)
                        sigmoid(gate_t, proj[:, half, :]).then_inc(bank_free[half], 1)
                        split_weights(pair, at + 2, half)
                    if last:
                        gate(pair, at + 1, 0, sg[:, 0, :], bank_free[0])
                    else:
                        store_k(pair, at + 1, 0)
                    weights(n)
                    if last:
                        gate(pair, at + 1, 1, sg[:, 1, :], bank_free[1])
                    else:
                        store_k(pair, at + 1, 1)
                    head_pair_out(n, ds(2 * g, 1))
                    logs(n + 1)
                    if last:
                        gate(pair, at + 2, 0, sg[:, 2, :], bank_free[0])
                        gate(pair, at + 2, 1, sg[:, 3, :], bank_free[1])
                        gate(pair, at + 3, 0, sg[:, 4, :], bank_free[0])
                    else:
                        store_v(pair, at + 2)
                        store_q(pair, at + 3, 0)
                    weights(n + 1)
                    if last:
                        gate(pair, at + 3, 1, sg[:, 5, :], bank_free[1])
                    else:
                        store_q(pair, at + 3, 1)
                    head_pair_out(n + 1, ds(2 * g + 1, 1))

                with own.loop(SB_GROUPS - 1, 8) as g:
                    group(first + 2 * g, g, SB_LOOP, False)
                group(first, SB_GROUPS - 1, SB_LAST, True)

                for half in range(2):
                    gate(first, GB_LAST, half, sg[:, 6 + half, :], bank_free[half])
                for m in range(4):
                    for half in range(2):
                        act.wait_ge(merged_sum, KT * layer + 2 * m + half + 1)
                        act.activation(h_hi[:, 2 * m + half, :], merged_t[:, half, :], ACT.Copy).then_inc(merged_half, 1)
                        split_weights(first, SB_OUT + m + 2, half)
                def added(pair, unit, half):
                    act.wait_ge(bank_free[half], 2 * pair + unit + 2)

                for m in range(4):
                    for half in range(2):
                        products(first, MIX + m, half)
                        split_weights(first, MIX + m + 2, half)
                        added(first, MIX + m, half)
                        square(2 * layer + 1, 2 * m + half, at_mlp)
                norm_affine(2 * layer + 1, at_mlp)

                def up(pair, f):
                    for m in range(4):
                        for half in range(2):
                            k = 2 * m + half
                            products(pair, MLP + m, half)
                            act.activation(relu_t[:, half, :], proj[:, half, :], ACT.Relu).then_inc(bank_free[half], 1)
                            act.wait_ge(u_ready, KT * (4 * layer + f) + k + 1)
                            act.activation(y_hi[:, k, :], u_t[:, half, :], ACT.Copy).then_inc(u_half, 1)
                            split_weights(pair, MLP + m + 2, half)

                def down(pair, last):
                    for m in range(4):
                        for half in range(2):
                            products(pair, MLP + 4 + m, half)
                            if not last or m < 2:
                                split_weights(pair, MLP + 4 + m + 2, half)
                            if last:
                                added(pair, MLP + 4 + m, half)
                                square(2 * layer + 2, 2 * m + half, at_layer)

                with own.loop(QUARTERS - 1, 0) as f:
                    up(first + 4 * f, f)
                    down(first + 4 * f, False)
                up(first + 4 * (QUARTERS - 1), QUARTERS - 1)
                down(first + 4 * (QUARTERS - 1), True)

            norm(2 * DEPTH, at_layer)
            for t in range(TB):
                act.wait_ge(y_turned, 2 * t + 2)
                act.activation(x_tok[:, t, SEQ:2 * SEQ], att[:, 2 * (t % 3) + 1, :], ACT.Copy).then_inc(y_stored, 1)

        @block.tensor
        def _(pe):
            n_rows = DEPTH * MODS * KT
            pe.wait_ge(consts_made, 10)
            pe.wait_ge(rows_in, 16)
            pe.wait_ge(consts_in, 64)
            pe.transpose(att[:, 0, 0:n_rows], rows[0:n_rows, :], ident[0:n_rows, 0:n_rows])
            pe.transpose(att[:, 0, n_rows:n_rows + 6 * KT], decay_t[0:6 * KT, 0:P],
                         ident[0:6 * KT, 0:6 * KT]).then_inc(vecs_turned, 1)
            pe.wait_ge(x_in, 16)
            for k in range(KT):
                if k == 0:
                    pe.wait_ge(vecs_ready, 1)
                if k >= 6:
                    pe.wait_ge(x_ready_dve if k % 2 == 0 else x_ready, 1)
                for t in range(TB):
                    last = pe.transpose(att[:, k % 6, t * P:(t + 1) * P], x_tok[:, t, k * P:(k + 1) * P], ident[:, :])
                last.then_inc(x_turned, 1)
            pe.wait_ge(c_ready, 1)
            for i, n in enumerate(FIRST_ON_PE):
                pe.wait_ge(first_in[n % 3], 16 * (n // 3 + 1))
                for j in range(2):
                    for k in range(KT):
                        last = pe.matmul(proj[:, 0, 2 * n + j:2 * n + j + 1],
                                         ada_first[:, n % 3, k, j * P:(j + 1) * P], c_act[:, k:k + 1],
                                         start=k == 0, stop=k == KT - 1)
                last.then_inc(ada_done, 1)
                for d in range(2 * i, min(2 * i + 2, len(FIRST_ON_DVE))):
                    pe.wait_ge(first_summed, d + 1)
                    for j in range(2):
                        at = 2 * FIRST_ON_DVE[d] + j
                        last = pe.matmul(proj[:, 0, at:at + 1], first_sum(d)[:, j * P:(j + 1) * P], one_c[:, :],
                                         start=True, stop=True)
                    last.then_inc(first_turned, 1)

            ada_pending = []

            def turn_ada():
                ada_pending.append(None)
                if len(ada_pending) > 2 and (due := ada_pending.pop(0)):
                    layer, n, n_slot = due
                    pe.wait_ge(ada_summed, ADA_UNITS * layer + n + 1 + 2)
                    for j in range(2):
                        last = pe.matmul(att[:, 1 + n_slot, j:j + 1], ada_sum[:, n_slot, j * P:(j + 1) * P],
                                         one_c[:, :], start=True, stop=True)
                    last.then_inc(ada_turned, 1)

            def half_unit(pair, unit, j, hi, lo, tile_ready=None):
                slot = 2 * (unit % 2) + j
                pe.wait_ge(lo_ready, 4 * pair + 2 * unit + j + 1 + LO_CREDIT)
                pe.wait_ge(bank_free[j], 2 * pair + unit + 1)
                for k in range(KT):
                    if tile_ready:
                        tile_ready(k)
                    for n, (w, a) in enumerate(((w_hi, hi), (w_hi, lo), (w_lo, hi))):
                        last = pe.matmul(proj[:, j, :], w[:, slot, k, :], a[:, k, :],
                                         start=k == 0 and n == 0, stop=k == KT - 1 and n == 2)
                last.then_inc(proj_done, 1)

            def whole_unit(pair, unit, hi, lo, tile_ready=None):
                for j in range(2):
                    half_unit(pair, unit, j, hi, lo, tile_ready if j == 0 else None)

            def first_unit(pair, unit, hi, lo, tile_ready, steps):
                k0 = 0
                for step in steps:
                    for j in range(2):
                        slot = 2 * (unit % 2) + j
                        if k0 == 0:
                            pe.wait_ge(lo_ready, 4 * pair + 2 * unit + j + 1 + LO_CREDIT)
                            pe.wait_ge(bank_free[j], 2 * pair + unit + 1)
                        for k in range(k0, k0 + step):
                            if j == 0:
                                tile_ready(k)
                            for n, (w, a) in enumerate(((w_hi, hi), (w_hi, lo), (w_lo, hi))):
                                last = pe.matmul(proj[:, j, :], w[:, slot, k, :], a[:, k, :],
                                                 start=k == 0 and n == 0, stop=k == KT - 1 and n == 2)
                        if k0 + step == KT:
                            last.then_inc(proj_done, 1)
                    k0 += step

            def token_unit(pair, unit):
                slot = 2 * (unit % 2)
                pe.wait_ge(lo_ready, 4 * pair + 2 * unit + 2 + LO_CREDIT)
                for t in range(TB):
                    if t % 2 == 0:
                        pe.wait_ge(bank_free[t // 2], 2 * pair + unit + 1)
                    for k in range(KT):
                        for n, (w, a) in enumerate(((w_hi, h_hi), (w_lo, h_hi), (w_hi, h_lo))):
                            last = pe.matmul(
                                proj[:, t // 2, UNIT * (t % 2):UNIT * (t % 2 + 1)].rearrange("p (a n) -> p a n", a=2),
                                a[:, k, t * P:(t + 1) * P], w[:, slot:slot + 2, k, :],
                                start=k == 0 and n == 0, stop=k == KT - 1 and n == 2)
                    if t % 2:
                        last.then_inc(proj_done, 1)

            def mean_square(n, buffers):
                pe.wait_ge(sq_used, 7 * n + 7)
                pe.matmul(att[:, 0, :], ones[:, :], buffers[1], start=True, stop=False)
                pe.wait_ge(squared, KT * n + KT)
                pe.matmul(att[:, 0, :], ones[:, :], buffers[0][:, 1, :], start=False, stop=True).then_inc(ms_done, 1)

            def normed_ready(n):
                return lambda k: pe.wait_ge(h_ready, KT * n + k + 1)

            with pe.Fori(0, DEPTH) as layer:
                first = layer * LAYER_PAIRS
                mean_square(2 * layer, at_layer)

                with pe.Fori(0, RET_LOOPS) as i:
                    pair = first + RET_PAIRS * i
                    for h in range(2):
                        head = 4 * layer + 2 * i + h
                        u = 6 * h
                        if h == 0:
                            first_unit(pair, u, h_hi, h_lo, normed_ready(2 * layer), BY_TILE)
                        else:
                            whole_unit(pair, u, h_hi, h_lo)
                        whole_unit(pair, u + 1, h_hi, h_lo)
                        token_unit(pair, u + 2)
                        token_unit(pair, u + 3)
                        pe.wait_ge(qk_rotated, 2 * head + 2)
                        for j in range(TB):
                            for half in range(2):
                                last = pe.matmul(att_flat[:, OFF[j]:OFF[j] + WID[j]],
                                                 qk[:, 2 + half, P * j:P * (j + 1)], qk[:, half, P * j:SEQ],
                                                 start=half == 0, stop=half == 1)
                        last.then_inc(scores_done, 1)
                        half_unit(pair, u + 4, 0, h_hi, h_lo)
                        pe.wait_ge(probs_ready, head + 1)
                        pe.wait_ge(bank_free[1], 2 * pair + u + 5)
                        for t in range(TB):
                            if t == 2:
                                half_unit(pair, u + 4, 1, h_hi, h_lo)
                            for j in range(t + 1):
                                at = OFF[j] + P * (t - j)
                                last = pe.matmul(att[:, RET_BANKS[t], :], p_ret[:, at:at + P], v_ret[:, j, :],
                                                 start=j == 0, stop=j == t)
                            last.then_inc(ret_done, 1)
                        half_unit(pair, u + 5, 0, h_hi, h_lo)
                        pe.wait_ge(ret_normed, 4 * head + TB)
                        for e in range(4):
                            for t in range(TB):
                                last = pe.transpose(att[:, TURNED_BANKS[e], P * t:P * (t + 1)],
                                                    qk[:, t, P * e:P * (e + 1)], ident[:, :])
                            last.then_inc(ret_turned, 1)
                        half_unit(pair, u + 5, 1, h_hi, h_lo)

                    def gated_ready(k):
                        pe.wait_ge(ret_gated, 4 * (4 * layer + 2 * i) + k + 1)

                    first_unit(pair, 12, y_hi, y_lo, gated_ready, (4, 4))
                    for m in range(1, 4):
                        whole_unit(pair, 12 + m, y_hi, y_lo)

                def scores(n, tile):
                    for j in range(TB):
                        if j == 2:
                            pe.wait_ge(sb_ready, n + 1)
                        for a in range(2):
                            r = slice(SB_DIM * a, SB_DIM * (a + 1))
                            at = 3 * a * SEQ + OFF[j]
                            last = pe.matmul(att_flat[:, at:at + WID[j]],
                                             tile2(sb_now, now_k)[r, tile, P * j:P * (j + 1)],
                                             tile2(sb_now, now_q)[r, tile, P * j:SEQ],
                                             start=j < 3, stop=True, skip_group_check=True)
                            if j == 3:
                                last.then_inc(z_done, 1)

                def break_stick(n):
                    for a in range(2):
                        pe.wait_ge(sp_ready, 2 * n + a + 1)
                        for i in range(TB):
                            for j in range(i, TB):
                                at = 3 * a * SEQ + OFF[i] + P * (j - i)
                                for sp_part in (sp_hi, sp_lo):
                                    last = pe.matmul(att_flat[:, at:at + WID[j]],
                                                     (neg_tri if i == j else neg_ones)[:, :],
                                                     sp_part[:, a, OFF[j]:OFF[j] + WID[j]],
                                                     start=False, stop=True, skip_group_check=True)
                        last.then_inc(broken, 1)

                def outputs(n, tile):
                    pe.wait_ge(weights_ready, 2 * n + 2)
                    for j in range(TB):
                        for a in range(2):
                            col = 2 * SB_DIM * tile + SB_DIM * a
                            last = pe.matmul(att[SB_DIM * a:SB_DIM * (a + 1), SB_OUT_BANK, P * j:SEQ],
                                             blocks(sb_now, now_v)[:, j, col:col + SB_DIM],
                                             terms[:, a, OFF[j]:OFF[j] + WID[j]],
                                             start=j == 0, stop=j == TB - 1, skip_group_check=True)
                    last.then_inc(sb_done, 1)

                whole_unit(first, SB_FIRST, h_hi, h_lo)
                token_unit(first, SB_FIRST + 1)
                whole_unit(first, SB_FIRST + 2, h_hi, h_lo)

                def group(pair, g, at, last):
                    n = 8 * layer + 2 * g
                    pe.wait_ge(qk_now, SB_GROUPS * layer + g + 1)
                    scores(n, 0)
                    whole_unit(pair, at, h_hi, h_lo)
                    half_unit(pair, at + 1, 0, h_hi, h_lo)
                    break_stick(n)
                    half_unit(pair, at + 1, 1, h_hi, h_lo)
                    pe.wait_ge(v_now, SB_GROUPS * layer + g + 1)
                    outputs(n, 0)
                    scores(n + 1, 1)
                    if last:
                        whole_unit(pair, at + 2, h_hi, h_lo)
                    else:
                        token_unit(pair, at + 2)
                    half_unit(pair, at + 3, 0, h_hi, h_lo)
                    break_stick(n + 1)
                    half_unit(pair, at + 3, 1, h_hi, h_lo)
                    outputs(n + 1, 1)

                with pe.Fori(0, SB_GROUPS - 1) as g:
                    group(first + 2 * g, g, SB_LOOP, False)
                group(first, SB_GROUPS - 1, SB_LAST, True)

                whole_unit(first, GB_LAST, h_hi, h_lo)
                for m in range(8):
                    hi, lo, unit = (y_hi, y_lo, SB_OUT + m) if m < 4 else (h_hi, h_lo, SB_OUT + m)
                    tile_ready = {0: lambda k: pe.wait_ge(sb_ready, 8 * layer + k + 2),
                                  4: lambda k: pe.wait_ge(merged_ready, KT * layer + k + 1)}.get(m)
                    for half in range(2):
                        half_unit(first, unit, half, hi, lo, tile_ready if half == 0 else None)
                        turn_ada()
                        n = ada_of(m, half)
                        if n is not None:
                            ada_pending[-1] = (layer, n, n % 2)
                mean_square(2 * layer + 1, at_mlp)

                def quarter(pair, f, with_ada):
                    for m in range(4):
                        if m == 0:
                            first_unit(pair, MLP, h_hi, h_lo, normed_ready(2 * layer + 1), BY_TILE)
                        for half in range(2):
                            if m > 0:
                                half_unit(pair, MLP + m, half, h_hi, h_lo)
                            turn_ada()
                            if with_ada and half == 0:
                                ada_pending[-1] = (layer, 4 * f + 12 + m, m % 2)
                    for m in range(4):
                        for half in range(2):
                            half_unit(pair, MLP + 4 + m, half, y_hi, y_lo,
                                      (lambda k: pe.wait_ge(u_split, KT * (4 * layer + f) + k + 1))
                                      if m == half == 0 else None)
                            turn_ada()

                with pe.Fori(0, QUARTERS - 1) as f:
                    quarter(first + 4 * f, f, True)
                quarter(first + 4 * (QUARTERS - 1), QUARTERS - 1, False)

            mean_square(2 * DEPTH, at_layer)
            for t in range(TB):
                for half in range(2):
                    bank = 2 * (t % 3) + half
                    if t == 3:
                        pe.wait_ge(y_stored if half else y_stored_dve, 1)
                    for k in range(4 * half, 4 * half + 4):
                        pe.wait_ge(x_normed, KT * 2 * DEPTH + k + 1)
                        last = pe.transpose(att[:, bank, P * (k % 4):P * (k % 4 + 1)], y_T[:, k, P * t:P * (t + 1)],
                                            ident[:, :])
                    last.then_inc(y_turned, 1)

        @block.vector
        def _(dve):
            own = Chain(dve, dve_own)
            own.mark(dve.memset(eps_c[:, :], EPS))
            own.mark(dve.memset(gn_eps_c[:, :], GN_EPS))
            own.mark(dve.memset(mod[:, DEPTH * MODS * KT:(DEPTH * MODS + 2) * KT], 0.0))
            for s in range(2):
                dve.sem_inc(bank_free[s], 1)
            dve.sem_inc(ada_summed, 2)
            dve.sem_inc(gate_used, 1)
            dve.sem_inc(sb_ready, 1)
            n_rows = DEPTH * MODS * KT
            dve.wait_ge(vecs_turned, 1)
            own.link(dve.tensor_copy(mod[:, 0:n_rows], att[:, 0, 0:n_rows]))
            dve.tensor_copy(vecs[:, :, :], att[:, 0, n_rows:n_rows + 6 * KT].rearrange("p (a b) -> p a b", a=6)
                            ).then_inc(vecs_ready, 1)
            dve.wait_ge(vecs_ready, 1)
            dve.wait_ge(c_sig, 1)
            dve.tensor_tensor(c_act[:, :], c_act[:, :], vecs[:, 0, :], ALU.mult).then_inc(c_ready, 1)
            def add_square(n, k, buffers):
                if 1 <= k <= KT - 2:
                    dve.wait_ge(squared, KT * n + k + 1)
                    if k >= 2:
                        dve.wait_ge(sq_used, 7 * n + k)
                    sq, sq_sum = buffers[0], buffers[1]
                    dve.tensor_tensor(sq_sum, sq[:, 0, :] if k == 1 else sq_sum, sq[:, k % 2, :],
                                      ALU.add).then_inc(sq_used, 2 if k == 1 else 1)

            def copy_x(k):
                dve.wait_ge(x_turned, k + 1)
                dve.tensor_copy(x_T[:, k, :], att[:, k % 6, :]).then_inc(x_ready_dve, 1)

            def weigh_rows(acc, raw, done):
                own.link(dve.tensor_scalar(acc, raw[:, 0, :], c_act[:, 0:1], None, ALU.mult))
                for k in range(1, KT):
                    ins = dve.scalar_tensor_tensor(acc, raw[:, k, :], c_act[:, k:k + 1], acc, ALU.mult, ALU.add)
                    if k < KT - 1:
                        own.link(ins)
                    else:
                        ins.then_inc(done, 1)

            dve.wait_ge(c_ready, 1)
            for d, n in enumerate(FIRST_ON_DVE):
                for k in ([0], [2], [4, 6], [], [])[d]:
                    copy_x(k)
                for k in ([], [], [1, 2], [3, 4], [5, 6])[d]:
                    add_square(0, k, at_layer)
                dve.wait_ge(first_in[n % 3], 16 * (n // 3 + 1))
                if d >= 4:
                    dve.wait_ge(first_turned, d - 3)
                weigh_rows(first_sum(d), ada_first[:, n % 3, :, :], first_summed)
            first_mods = 2 * KT
            dve.wait_ge(ada_done, len(FIRST_ON_PE))
            dve.wait_ge(first_turned, len(FIRST_ON_DVE))
            own.link(dve.tensor_tensor(mod[:, 0:first_mods], mod[:, 0:first_mods], proj[:, 0, 0:first_mods], ALU.add))

            def scale_and_shift(layer, which):
                n = 2 * layer + which
                shift = layer * (MODS * KT) + KT * (SHIFT1, SHIFT2)[which]
                gain = vecs[:, 1 + DEPTH * which:1 + DEPTH * (which + 1), :].rearrange("p a b -> p (a b)")
                own.mark(dve.scalar_tensor_tensor(n_scale[:, ds(KT * n, KT)], mod[:, ds(shift + KT, KT)], 1.0,
                                                  gain[:, ds(layer * KT, KT)], ALU.add, ALU.mult))
                dve.tensor_copy(n_shift[:, ds(KT * n, KT)], mod[:, ds(shift, KT)]).then_inc(mods_ready, 1)

            def sum_ada(layer, n, slot, pair_of):
                dve.wait_ge(ada_in[slot], 16 * (ADA_UNITS // 2 * layer + pair_of + 1))
                weigh_rows(ada_sum[:, slot, :], ada_raw[:, slot, :, :], ada_summed)

            def take_ada(layer, n, slot):
                dve.wait_ge(ada_turned, ADA_UNITS * layer + n + 1)
                at = ds((layer * MODS + 2) * KT + 2 * n, 2)
                own.link(dve.tensor_tensor(mod[:, at], mod[:, at], att[:, 1 + slot, 0:2], ALU.add))

            def products(pair, unit, half):
                dve.wait_ge(proj_done, 4 * pair + 2 * unit + half + 1)

            def taken(pair, unit, half):
                dve.wait_ge(bank_free[half], 2 * pair + unit + 2)

            def free(ins, half):
                ins.then_inc(bank_free[half], 1)

            def norm(n, buffers):
                dst = buffers[3]
                dve.wait_ge(mods_ready, n + 1)
                dve.wait_ge(rstd_ready, n + 1)
                for k in range(KT + 1):
                    if k < KT:
                        if k >= 2:
                            dve.wait_ge(h_ready, KT * n + k - 1)
                        dve.scalar_tensor_tensor(dst[:, k % 2, :], x_T[:, k, :], n_scale[:, ds(KT * n + k, 1)],
                                                 buffers[2], ALU.mult, ALU.mult).then_inc(x_normed, 1)
                    if k >= 1:
                        dve.wait_ge(h_half, KT * n + k)
                        dve.scalar_tensor_tensor(h_lo[:, k - 1, :], dst[:, (k - 1) % 2, :],
                                                 n_shift[:, ds(KT * n + k - 1, 1)], h_hi[:, k - 1, :],
                                                 ALU.add, ALU.subtract).then_inc(h_ready, 1)

            def add_to_x(pair, unit, half, k, gate_col):
                products(pair, unit, half)
                free(dve.scalar_tensor_tensor(x_T[:, k, :], proj[:, half, :], mod[:, ds(gate_col + k, 1)],
                                              x_T[:, k, :], ALU.mult, ALU.add), half)

            with own.loop(DEPTH, 326) as layer:
                first = layer * LAYER_PAIRS
                dve.wait_ge(x_turned, KT)
                dve.memset(ya[:, :, :], 0.0)
                scale_and_shift(layer, 0)
                norm(2 * layer, at_layer)
                with own.loop(RET_LOOPS, 42) as i:
                    pair = first + RET_PAIRS * i
                    for h in range(2):
                        head = 4 * layer + 2 * i + h
                        u = 6 * h
                        dve.wait_ge(rope_in, 16 * layer + 16)
                        for n in range(2):
                            a, b = qk[:, 2 * n, :], qk[:, 2 * n + 1, :]
                            products(pair, u + n, 0)
                            dve.tensor_tensor(a, proj[:, 0, :], rope_t[:, 0, :], ALU.mult)
                            free(dve.tensor_tensor(b, proj[:, 0, :], rope_t[:, 1, :], ALU.mult), 0)
                            products(pair, u + n, 1)
                            own.link(dve.tensor_tensor(rot, proj[:, 1, :], rope_t[:, 1, :], ALU.mult))
                            own.link(dve.tensor_tensor(a, a, rot, ALU.subtract))
                            free(dve.tensor_tensor(rot, proj[:, 1, :], rope_t[:, 0, :], ALU.mult), 1)
                            dve.wait_ge(bank_free[1], 2 * pair + u + n + 2)
                            dve.tensor_tensor(b, b, rot, ALU.add).then_inc(qk_rotated, 1)
                            dve.wait_ge(qk_rotated, 2 * head + n + 1)
                        dve.wait_ge(decay_in, 16 * head + 16)
                        dve.wait_ge(scores_done, head + 1)
                        for j in (0, 1, 3, 2):
                            ins = dve.tensor_tensor(p_ret[:, OFF[j]:OFF[j] + WID[j]], att_flat[:, OFF[j]:OFF[j] + WID[j]],
                                                    decay_t[:, 0:WID[j]], ALU.mult)
                        ins.then_inc(probs_ready, 1)

                        def silu(n):
                            dve.wait_ge(sig_ready, 4 * head + n + 1)
                            free(dve.tensor_tensor(g_ret[:, n, :], g_ret[:, n, :], proj[:, n % 2, :], ALU.mult), n % 2)

                        def moments_of(t):
                            dve.wait_ge(ret_done, 4 * head + t + 1)
                            own.mark(dve.bn_stats(stats[:, t, :], att[:, RET_BANKS[t], :]))

                        silu(0)
                        moments_of(0)
                        moments_of(1)
                        silu(1)
                        moments_of(2)
                        moments_of(3)
                        own.settle()
                        own.mark(dve.tensor_tensor(mean_diff[:, :], stats[:, :, 1], stats[:, :, 4], ALU.subtract))
                        own.mark(dve.tensor_tensor(moments[:, :, 0], stats[:, :, 1], stats[:, :, 4], ALU.add))
                        own.link(dve.tensor_tensor(moments[:, :, 1], stats[:, :, 2], stats[:, :, 5], ALU.add))
                        own.link(dve.scalar_tensor_tensor(mean_diff[:, :], mean_diff[:, :], RET_V / 4.0,
                                                          mean_diff[:, :], ALU.mult, ALU.mult))
                        own.link(dve.tensor_scalar(moments[:, :, 0], moments[:, :, 0], 0.5, None, ALU.mult))
                        dve.tensor_tensor(moments[:, :, 1], moments[:, :, 1], mean_diff[:, :],
                                          ALU.add).then_inc(moments_ready, 1)
                        dve.wait_ge(ret_rstd_ready, head + 1)
                        for t in range(TB):
                            dve.tensor_scalar(qk[:, t, :], att[:, RET_BANKS[t], :], moments[:, t, 0:1],
                                              ret_rstd[:, t:t + 1], ALU.subtract, ALU.mult).then_inc(ret_normed, 1)
                        silu(2)
                        taken(pair, u + 5, 0)
                        for e in range(4):
                            if e == 3:
                                silu(3)
                                taken(pair, u + 5, 1)
                            dve.wait_ge(ret_turned, 4 * head + e + 1)
                            own.link(dve.tensor_tensor(gated_t, g_ret[:, e, :], att[:, TURNED_BANKS[e], :], ALU.mult))
                            own.link(dve.tensor_copy(y_hi[:, 4 * h + e, :], gated_t))
                            dve.tensor_tensor(y_lo[:, 4 * h + e, :], gated_t, y_hi[:, 4 * h + e, :],
                                              ALU.subtract).then_inc(ret_gated, 1)
                            dve.wait_ge(ret_gated, 4 * head + e + 1)
                    for m in range(4):
                        for half in range(2):
                            products(pair, 12 + m, half)
                            k = 2 * m + half
                            free(dve.tensor_tensor(ya[:, k, :], ya[:, k, :], proj[:, half, :], ALU.add), half)

                def mask(buf):
                    three = buf[:, 0:3 * SEQ - 2 * P].rearrange("p (j n) -> p j n", n=P)[:, 0:9:4, :]
                    dve.tensor_tensor(three, three, upto[:, :].rearrange("p (a n) -> p a n", a=1).to_broadcast([P, 3, P]),
                                      ALU.min)
                    one = buf[:, OFF[3]:OFF[3] + P]
                    return dve.tensor_tensor(one, one, upto[:, :], ALU.min)

                def softplus(n):
                    for a in range(2):
                        dve.wait_ge(log_ready, 2 * n + a + 1)
                        own.link(dve.scalar_tensor_tensor(terms[:, a, :], scores_of(a), 0.0, terms[:, a, :],
                                                          ALU.max, ALU.add))
                        own.link(mask(terms[:, a, :]))
                        own.link(dve.tensor_copy(sp_hi[:, a, :], terms[:, a, :]))
                        dve.tensor_tensor(sp_lo[:, a, :], terms[:, a, :], sp_hi[:, a, :],
                                          ALU.subtract).then_inc(sp_ready, 1)

                def mask_weights(n):
                    for a in range(2):
                        dve.wait_ge(weights_exp, 2 * n + a + 1)
                        mask(terms[:, a, :]).then_inc(weights_ready, 1)

                def low_output(n, tile):
                    dve.wait_ge(sb_half, n + 1)
                    dve.tensor_tensor(y_lo[:, tile, :], att[:, SB_OUT_BANK:SB_OUT_BANK + 1, :], y_hi[:, tile, :],
                                      ALU.subtract).then_inc(sb_ready, 1)

                def take_qk(pair, unit):
                    taken(pair, unit, 1)
                    for part_of in (now_k, now_q):
                        ins = dve.tensor_copy(sb_now[:, part_of, :], sb_next[:, part_of, :])
                    ins.then_inc(qk_now, 1)

                def take_v():
                    dve.tensor_copy(sb_now[:, now_v, :], sb_next[:, now_v, :]).then_inc(v_now, 1)

                take_qk(first, SB_FIRST + 2)
                take_v()

                def group(pair, g, at, last):
                    n = 8 * layer + 2 * g
                    softplus(n)
                    for half in range(2):
                        taken(pair, at, half)
                        dve.tensor_tensor(ya[:, ds(2 * g + half, 1), :], ya[:, ds(2 * g + half, 1), :],
                                          gate_t.rearrange("p (a n) -> p a n", a=1), ALU.mult).then_inc(gate_used, 1)
                    mask_weights(n)
                    low_output(n, ds(2 * g, 1))
                    softplus(n + 1)
                    mask_weights(n + 1)
                    if not last:
                        take_qk(pair, at + 3)
                    low_output(n + 1, ds(2 * g + 1, 1))
                    if not last:
                        take_v()

                with own.loop(SB_GROUPS - 1, 12) as g:
                    group(first + 2 * g, g, SB_LOOP, False)
                group(first, SB_GROUPS - 1, SB_LAST, True)

                gates = MODS * KT * layer
                pending = []

                def due_ada():
                    pending.append(None)
                    if len(pending) > 2 and (due := pending.pop(0)):
                        take_ada(*due)

                for m in range(8):
                    for half in range(2):
                        k = 2 * (m % 4) + half
                        if m < 4:
                            products(first, SB_OUT + m, half)
                            free(dve.tensor_tensor(merged_t[:, half, :], proj[:, half, :], sg[:, k, :], ALU.mult), half)
                            taken(first, SB_OUT + m, half)
                            dve.tensor_tensor(merged_t[:, half, :], merged_t[:, half, :], ya[:, k, :],
                                              ALU.add).then_inc(merged_sum, 1)
                            dve.wait_ge(merged_half, KT * layer + k + 1)
                            dve.tensor_tensor(h_lo[:, k, :], merged_t[:, half, :], h_hi[:, k, :],
                                              ALU.subtract).then_inc(merged_ready, 1)
                        else:
                            add_square(2 * layer + 1, k - 1, at_mlp)
                            add_to_x(first, SB_OUT + m, half, k, gates + KT * GATE1)
                        due_ada()
                        n = ada_of(m, half)
                        if n is not None:
                            sum_ada(layer, n, n % 2, n // 2)
                            pending[-1] = (layer, n, n % 2)
                scale_and_shift(layer, 1)
                norm(2 * layer + 1, at_mlp)

                def quarter(pair, f, last):
                    for m in range(4):
                        for half in range(2):
                            k = 2 * m + half
                            n = KT * (4 * layer + f) + k
                            taken(pair, MLP + m, half)
                            dve.tensor_tensor(u_t[:, half, :], relu_t[:, half, :], relu_t[:, half, :],
                                              ALU.mult).then_inc(u_ready, 1)
                            dve.wait_ge(u_half, n + 1)
                            dve.tensor_tensor(y_lo[:, k, :], u_t[:, half, :], y_hi[:, k, :],
                                              ALU.subtract).then_inc(u_split, 1)
                            due_ada()
                            if half == 0 and not last:
                                n = 4 * f + 12 + m
                                sum_ada(layer, n, m % 2, 2 * f + 6 + m // 2)
                                pending[-1] = (layer, n, m % 2)
                    for m in range(4):
                        for half in range(2):
                            k = 2 * m + half
                            if last:
                                add_square(2 * layer + 2, k - 1, at_layer)
                            add_to_x(pair, MLP + 4 + m, half, k, gates + KT * GATE2)
                            due_ada()

                with own.loop(QUARTERS - 1, 32) as f:
                    quarter(first + 4 * f, f, False)
                quarter(first + 4 * (QUARTERS - 1), QUARTERS - 1, True)

            dve.wait_ge(rstd_ready, 2 * DEPTH + 1)
            for k in range(KT):
                dve.scalar_tensor_tensor(y_T[:, k, :], x_T[:, k, :], vecs[:, 5, k:k + 1], at_layer[2],
                                         ALU.mult, ALU.mult).then_inc(x_normed, 1)
            for t in range(TB):
                dve.wait_ge(y_turned, 2 * t + 1)
                dve.tensor_copy(x_tok[:, t, 0:SEQ], att[:, 2 * (t % 3), :]).then_inc(y_stored_dve, 1)


def rope_tables():
    half = RET_QK // 2
    inv_freq = np.power(np.float32(10000.0), -np.arange(half, dtype=np.float32) / np.float32(half))
    angle = inv_freq[:, None] * np.arange(SEQ, dtype=np.float32)[None, :]
    return np.stack([np.cos(angle), np.sin(angle)], axis=1).astype(np.float32)


def decay_tables():
    gamma = 1.0 - 2.0 ** (-5.0 - np.arange(RET_HEADS))
    rel = np.arange(SEQ)[None, None, :] - np.arange(P)[:, None, None]
    table = np.where(rel >= 0, gamma[None, :, None] ** np.maximum(rel, 0), 0.0) * RET_QK ** -0.5
    return table.astype(np.float32)


_INS = ["x", "c", "norm_mix_g", "w_in", "w_ret_out", "w_sb_out", "w_mix_out", "norm_mlp_g",
        "w_up", "w_down", "w_ada", "b_ada", "final_g"]


def kernel(**inputs):
    import concourse.bacc as bacc
    from concourse.bass_utils import run_bass_kernel_spmd

    nc = bacc.Bacc("TRN2", target_bir_lowering=False, num_devices=1)
    arrays = {name: np.ascontiguousarray(inputs[name]) for name in _INS}
    arrays["rope"] = rope_tables()
    arrays["decay"] = decay_tables()
    args = [nc.dram_tensor(f"in_{name}", a.shape, mybir.dt.from_np(a.dtype), kind="ExternalInput").ap()
            for name, a in arrays.items()]
    out = nc.dram_tensor("out", inputs["x"].shape, mybir.dt.float32, kind="ExternalOutput").ap()
    hybrid_trunk(nc, *args, out)
    result = run_bass_kernel_spmd(nc, [{f"in_{name}": a for name, a in arrays.items()}], core_ids=[0])
    return result.results[0]["out"]
```
